# Optimizing a Trainium2 kernel written in Bass

```python
import jax, jax.numpy as jnp
from jax import lax
import numpy as np

D_MODEL = 2048
BATCH = 1
SEQ = 512
DEPTH = 1

HEAD_DIM = 128
N_DELTA_HEADS = D_MODEL // (2 * HEAD_DIM)
N_ATTN_HEADS = D_MODEL // (2 * HEAD_DIM)
DELTA_WIDTH = N_DELTA_HEADS * HEAD_DIM
ATTN_WIDTH = N_ATTN_HEADS * HEAD_DIM
MIX_WIDTH = DELTA_WIDTH + ATTN_WIDTH
CONV_WIDTH = 4
CHUNK = 64
DILATED_PATTERNS = ((128, 1), (512, 4), (2048, 16))
ROPE_THETA = 10000.0
D_FF = ((8 * D_MODEL // 3 + 255) // 256) * 256
EPS = 1e-6

PROJ_SIZES = (DELTA_WIDTH, DELTA_WIDTH, DELTA_WIDTH, DELTA_WIDTH, N_DELTA_HEADS, N_DELTA_HEADS,
              ATTN_WIDTH, ATTN_WIDTH, ATTN_WIDTH)
PROJ_WIDTH = int(sum(PROJ_SIZES))
SPLIT_POINTS = tuple(int(s) for s in np.cumsum(PROJ_SIZES)[:-1])

kernel_name = "hybrid_deltanet_dilated_swa_layer"

def rms_norm(x, w):
    xf = x.astype(jnp.float32)
    y = xf * lax.rsqrt(jnp.mean(xf * xf, axis=-1, keepdims=True) + EPS)
    return (y * w.astype(jnp.float32)).astype(x.dtype)

def l2_norm(x):
    xf = x.astype(jnp.float32)
    return xf * lax.rsqrt(jnp.sum(xf * xf, axis=-1, keepdims=True) + EPS)

def rope(x, positions):
    half = x.shape[-1] // 2
    inv_freq = ROPE_THETA ** (-jnp.arange(half, dtype=jnp.float32) / half)
    ang = positions.astype(jnp.float32)[..., None] * inv_freq
    cos = jnp.cos(ang)[:, :, None, :]
    sin = jnp.sin(ang)[:, :, None, :]
    xf = x.astype(jnp.float32)
    x1, x2 = xf[..., :half], xf[..., half:]
    return jnp.concatenate([x1 * cos - x2 * sin, x2 * cos + x1 * sin], axis=-1).astype(x.dtype)

def causal_depthwise_conv_silu(x, w):
    k_len, chans = w.shape
    y = lax.conv_general_dilated(x, w[:, None, :].astype(x.dtype), window_strides=(1,),
                                 padding=[(k_len - 1, 0)],
                                 dimension_numbers=('NWC', 'WIO', 'NWC'),
                                 feature_group_count=chans)
    return jax.nn.silu(y)

def gated_delta_rule_chunked(q, k, v, g, beta):
    bsz, seq, heads, dk = q.shape
    dv = v.shape[-1]
    n = seq // CHUNK
    def to_chunks(t):
        return t.reshape(bsz, n, CHUNK, heads, t.shape[-1]).transpose(0, 3, 1, 2, 4)
    qc, kc, vc = to_chunks(q), to_chunks(k), to_chunks(v)
    gc = jnp.cumsum(g.reshape(bsz, n, CHUNK, heads).transpose(0, 3, 1, 2), axis=-1)
    bc = beta.reshape(bsz, n, CHUNK, heads).transpose(0, 3, 1, 2)
    idx = jnp.arange(CHUNK)
    causal = idx[:, None] >= idx[None, :]
    strict = idx[:, None] > idx[None, :]
    diff = gc[..., :, None] - gc[..., None, :]
    decay = jnp.where(causal, jnp.exp(jnp.where(causal, diff, 0.0)), 0.0)
    kk = jnp.einsum('bhncd,bhnmd->bhncm', kc, kc)
    lower = jnp.where(strict, bc[..., :, None] * kk * decay, 0.0)
    a_mat = lower + jnp.eye(CHUNK, dtype=jnp.float32)
    rhs = jnp.concatenate([vc * bc[..., None], kc * (bc * jnp.exp(gc))[..., None]], axis=-1)
    sol = lax.linalg.triangular_solve(a_mat, rhs, left_side=True, lower=True, unit_diagonal=True)
    u, w = sol[..., :dv], sol[..., dv:]
    qk = jnp.einsum('bhncd,bhnmd->bhncm', qc, kc) * decay
    q_dec = qc * jnp.exp(gc)[..., None]
    k_dec = kc * jnp.exp(gc[..., -1:] - gc)[..., None]
    chunk_decay = jnp.exp(gc[..., -1])

    def step(state, xs):
        u_c, w_c, qk_c, qd_c, kd_c, dec_c = xs
        v_new = u_c - jnp.einsum('bhcd,bhde->bhce', w_c, state)
        o_c = jnp.einsum('bhcd,bhde->bhce', qd_c, state) + jnp.einsum('bhcm,bhme->bhce', qk_c, v_new)
        state = state * dec_c[..., None, None] + jnp.einsum('bhcd,bhce->bhde', kd_c, v_new)
        return state, o_c

    xs = tuple(jnp.moveaxis(t, 2, 0) for t in (u, w, qk, q_dec, k_dec, chunk_decay))
    state0 = jnp.zeros((bsz, heads, dk, dv), jnp.float32)
    _, o = lax.scan(step, state0, xs)
    return o.transpose(1, 0, 3, 2, 4).reshape(bsz, seq, heads, dv)

def dilated_window_branch(q, k, v, window, dilation):
    bsz, seq, heads, hd = q.shape
    span = window // dilation
    blk = span
    unit = dilation * blk
    s_pad = -(-seq // unit) * unit
    nb = s_pad // unit
    def to_blocks(t):
        t = jnp.pad(t, [(0, 0), (0, s_pad - seq), (0, 0), (0, 0)])
        return t.reshape(bsz, nb, blk, dilation, heads, hd)
    def with_prev(t):
        prev = jnp.pad(t, [(0, 0), (1, 0), (0, 0), (0, 0), (0, 0), (0, 0)])[:, :-1]
        return jnp.concatenate([prev, t], axis=2)
    qb = to_blocks(q)
    kw = with_prev(to_blocks(k))
    vw = with_prev(to_blocks(v))
    s = jnp.einsum('bnqrhd,bnkrhd->bnrhqk', qb, kw,
                   preferred_element_type=jnp.float32) * (hd ** -0.5)
    qi = jnp.arange(blk)[:, None]
    ki = jnp.arange(2 * blk)[None, :]
    dist = qi + blk - ki
    band = (dist >= 0) & (dist <= span)
    mask = band[None] & ((jnp.arange(nb)[:, None, None] > 0) | (ki[None] >= blk))
    s = jnp.where(mask[None, :, None, None], s, -jnp.inf)
    m = jnp.max(s, axis=-1)
    p = jnp.exp(s - m[..., None])
    den = jnp.sum(p, axis=-1)
    o = jnp.einsum('bnrhqk,bnkrhd->bnqrhd', p, vw.astype(jnp.float32))
    m = m.transpose(0, 1, 4, 2, 3)
    den = den.transpose(0, 1, 4, 2, 3)
    o = o / den[..., None]
    o = o.reshape(bsz, s_pad, heads, hd)[:, :seq]
    m = m.reshape(bsz, s_pad, heads)[:, :seq]
    den = den.reshape(bsz, s_pad, heads)[:, :seq]
    return o, m, den

def dilated_mixture_attention(q, k, v):
    branches = [dilated_window_branch(q, k, v, w, d) for (w, d) in DILATED_PATTERNS]
    m_all = branches[0][1]
    for _, m_i, _ in branches[1:]:
        m_all = jnp.maximum(m_all, m_i)
    num = 0.0
    tot = 0.0
    for o_i, m_i, den_i in branches:
        wt = den_i * jnp.exp(m_i - m_all)
        num = num + wt[..., None] * o_i
        tot = tot + wt
    return num / tot[..., None]

def setup_inputs(seed: int = 0) -> dict:
    key = jax.random.key(seed)
    ks = jax.random.split(key, 20)
    f32 = jnp.float32
    x = jax.random.normal(ks[0], (BATCH, SEQ, D_MODEL), f32)
    offset = jax.random.randint(ks[1], (BATCH, 1), 0, 1024, dtype=jnp.int32)
    positions = (offset + jnp.arange(SEQ, dtype=jnp.int32)[None, :]).astype(jnp.int32)
    def gain(k, n):
        return 1.0 + 0.02 * jax.random.normal(k, (DEPTH, n), f32)
    attn_norm_w = gain(ks[2], D_MODEL)
    w_in = jax.random.normal(ks[3], (DEPTH, D_MODEL, PROJ_WIDTH), f32) * D_MODEL ** -0.5
    conv_w = jax.random.normal(ks[4], (DEPTH, CONV_WIDTH, 3 * DELTA_WIDTH), f32) * CONV_WIDTH ** -0.5
    a_log = jnp.log(jax.random.uniform(ks[5], (DEPTH, N_DELTA_HEADS), f32, 1.0, 16.0))
    dt = jnp.exp(jax.random.uniform(ks[6], (DEPTH, N_DELTA_HEADS), f32, np.log(1e-3), np.log(1e-1)))
    dt_bias = dt + jnp.log(-jnp.expm1(-dt))
    delta_out_norm_w = gain(ks[7], HEAD_DIM)
    q_norm_w = gain(ks[8], HEAD_DIM)
    k_norm_w = gain(ks[9], HEAD_DIM)
    attn_out_norm_w = gain(ks[10], HEAD_DIM)
    w_out = jax.random.normal(ks[11], (DEPTH, MIX_WIDTH, D_MODEL), f32) * MIX_WIDTH ** -0.5
    ffn_norm_w = gain(ks[12], D_MODEL)
    w_gate_up = jax.random.normal(ks[13], (DEPTH, D_MODEL, 2 * D_FF), f32) * D_MODEL ** -0.5
    w_down = jax.random.normal(ks[14], (DEPTH, D_FF, D_MODEL), f32) * D_FF ** -0.5
    return {'x': x, 'positions': positions, 'attn_norm_w': attn_norm_w, 'w_in': w_in,
            'conv_w': conv_w, 'a_log': a_log, 'dt_bias': dt_bias,
            'delta_out_norm_w': delta_out_norm_w, 'q_norm_w': q_norm_w, 'k_norm_w': k_norm_w,
            'attn_out_norm_w': attn_out_norm_w, 'w_out': w_out, 'ffn_norm_w': ffn_norm_w,
            'w_gate_up': w_gate_up, 'w_down': w_down}

def reference(x, positions, attn_norm_w, w_in, conv_w, a_log, dt_bias, delta_out_norm_w,
              q_norm_w, k_norm_w, attn_out_norm_w, w_out, ffn_norm_w, w_gate_up, w_down):
    bsz, seq, _ = x.shape
    for l in range(DEPTH):
        h = rms_norm(x, attn_norm_w[l])
        proj = h @ w_in[l].astype(h.dtype)
        qkv_raw, dz, db, da, aq, ak, av = jnp.split(
            proj, [3 * DELTA_WIDTH] + list(SPLIT_POINTS[3:]), axis=-1)
        qkv = causal_depthwise_conv_silu(qkv_raw, conv_w[l])
        dq, dk, dv = jnp.split(qkv, 3, axis=-1)
        dq = l2_norm(dq.reshape(bsz, seq, N_DELTA_HEADS, HEAD_DIM)) * (HEAD_DIM ** -0.5)
        dk = l2_norm(dk.reshape(bsz, seq, N_DELTA_HEADS, HEAD_DIM))
        dv = dv.reshape(bsz, seq, N_DELTA_HEADS, HEAD_DIM).astype(jnp.float32)
        beta = jax.nn.sigmoid(db.astype(jnp.float32))
        g = -jnp.exp(a_log[l].astype(jnp.float32)) * jax.nn.softplus(
            da.astype(jnp.float32) + dt_bias[l].astype(jnp.float32))
        o_a = gated_delta_rule_chunked(dq, dk, dv, g, beta)
        z = dz.reshape(bsz, seq, N_DELTA_HEADS, HEAD_DIM).astype(jnp.float32)
        o_a = (rms_norm(o_a, delta_out_norm_w[l]) * jax.nn.silu(z)).astype(x.dtype)
        aq = rope(rms_norm(aq.reshape(bsz, seq, N_ATTN_HEADS, HEAD_DIM), q_norm_w[l]), positions)
        ak = rope(rms_norm(ak.reshape(bsz, seq, N_ATTN_HEADS, HEAD_DIM), k_norm_w[l]), positions)
        av = av.reshape(bsz, seq, N_ATTN_HEADS, HEAD_DIM)
        o_b = dilated_mixture_attention(aq, ak, av)
        o_b = rms_norm(o_b, attn_out_norm_w[l]).astype(x.dtype)
        mixed = jnp.concatenate([o_a.reshape(bsz, seq, DELTA_WIDTH),
                                 o_b.reshape(bsz, seq, ATTN_WIDTH)], axis=-1)
        x = x + mixed @ w_out[l].astype(x.dtype)
        h = rms_norm(x, ffn_norm_w[l])
        gate, up = jnp.split(h @ w_gate_up[l].astype(h.dtype), 2, axis=-1)
        x = x + (jax.nn.silu(gate) * up) @ w_down[l].astype(x.dtype)
    return x


_drawn_inputs = setup_inputs


def setup_inputs(seed=0):
    import zlib

    import numpy as np

    out = dict(_drawn_inputs(seed))
    spreads = {}
    factors = {'delta_out_norm_w': 7.891,
     'q_norm_w': 4.901,
     'k_norm_w': 4.591,
     'attn_out_norm_w': 4.178,
     'ffn_norm_w': 4.8}
    for name, (base, spread) in spreads.items():
        noise = np.random.default_rng([zlib.crc32(name.encode()), seed]).standard_normal(out[name].shape)
        drawn = base * np.exp(spread * noise) if base else spread * noise
        out[name] = __import__('jax').numpy.asarray(drawn.astype(out[name].dtype))
    for name, factor in factors.items():
        out[name] = (out[name] * factor).astype(out[name].dtype)
    return out
```

```python
from contextlib import ExitStack

import numpy as np

import concourse.bass as bass
from concourse import mybir

F32 = mybir.dt.float32
F32R = mybir.dt.float32r
I32 = mybir.dt.int32
ACT = mybir.ActivationFunctionType
ALU = mybir.AluOpType
AXX = mybir.AxisListType.X

P = 128
SEQ = 512
TT_N = SEQ // P
DM = 2048
KT = DM // P
HEADS = 8
GW = HEADS * P
CONV = 4
FF = ((8 * DM // 3 + 255) // 256) * 256
FT = FF // P
FG = 4
FPG = FT // FG
EPS = 1e-6
SCALE = float(P) ** -0.5
THETA = 10000.0
LEVELS = [2, 4, 8, 16, 32, 64]
NL = len(LEVELS)
NEG = -1e30
DILATED = ((128, 1), (512, 4), (2048, 16))

C_ID, C_U, C_SL, C_NM1, C_MQ = 0, P, 2 * P, 3 * P, 4 * P
C_CNT = C_MQ + NL * P
C_NEG = C_CNT + SEQ
C_FREQ = C_NEG + SEQ
C_END = C_FREQ + P // 2

RING = 4
UNIT = 512
AHEAD = 3
A_N = 3 * P
D_KT = 4
A_UNITS = KT
D_UNITS = 4 * KT // D_KT
H_UNITS = A_UNITS + D_UNITS
O_UNITS = 4 * KT
GU_UNITS = 2 * KT // D_KT
DN_UNITS = 4 * FPG
F_UNITS = FPG * GU_UNITS + DN_UNITS
U_OUT = HEADS * H_UNITS
U_FFN = U_OUT + O_UNITS

BETA, GC, EG, BEG, EKD, DEC, G_ = range(7)

A_STAGES = {0: ["d_tokens", "a_sq"], 3: ["d_khat"], 4: ["d_kk"], 5: ["a_tail"], 6: ["d_ti"], 7: ["q0"],
            8: ["u0"], 9: ["q1"], 10: ["u1"], 11: ["q2"], 12: ["u2"], 13: ["q3"], 14: ["u3"], 15: ["q4", "a_evac"]}
D_STAGES = {0: ["u4", "a_norm"], 1: ["q5", "a_sum"], 2: ["u5"], 3: ["d_wt", "conv0"], 4: ["v0"],
            5: ["r0", "a_turn"], 6: ["a_score0", "v1"], 7: ["conv1", "a_prob0", "r1"], 8: ["a_pv0", "a_score1", "v2"],
            9: ["a_prob1", "r2"], 10: ["a_pv1", "a_score2", "v3"], 11: ["conv2", "a_prob2", "r3"],
            12: ["a_pv2", "a_score3", "d_norm"], 13: ["a_prob3"], 14: ["a_pv3", "d_turn"], 15: ["a_out", "conv3"]}


SMALL = 11
DVE_SIN, DVE_DB, DVE_ABS, DVE_G, DVE_EXPS, DVE_BEG = 17, 18, 21, 24, 27, 28


def constants():
    c = np.zeros((P, C_END), np.float32)
    i, j = np.arange(P)[:, None], np.arange(P)[None, :]
    c[:, C_ID:C_ID + P] = i == j
    c[:, C_U:C_U + P] = i <= j
    c[:, C_SL:C_SL + P] = i > j
    c[:, C_NM1:C_NM1 + P] = -1.0 * ((i // 2 == j // 2) & (i > j))
    for n, b in enumerate(LEVELS):
        o = C_MQ + n * P
        c[:, o:o + P] = (i // (2 * b) == j // (2 * b)) & ((i // b) % 2 == 0) & ((j // b) % 2 == 1)
    for block in range(TT_N):
        dist = (TT_N - 1 - block) * P + i - j
        count = np.zeros((P, P), np.float32)
        for window, step in DILATED:
            count += (dist >= 0) & (dist <= window) & (dist % step == 0)
        c[:, C_CNT + block * P:C_CNT + (block + 1) * P] = count
        c[:, C_NEG + block * P:C_NEG + (block + 1) * P] = np.where(count > 0, 0.0, NEG)
    half = P // 2
    c[:, C_FREQ:] = (np.float32(THETA) ** (-np.arange(half, dtype=np.float32) / np.float32(half)))[None, :]
    return c


def hybrid_layer(nc, x, positions, attn_norm_w, w_in, conv_w, a_log, dt_bias, delta_out_norm_w, q_norm_w,
                 k_norm_w, attn_out_norm_w, w_out, ffn_norm_w, w_gate_up, w_down, cst, out):
    ctx = ExitStack()

    def sb(name, shape, dt=F32, stack=ctx):
        return stack.enter_context(nc.sbuf_tensor(name, shape, dt))

    def sem(name):
        return ctx.enter_context(nc.semaphore(name))

    with ctx:
        bank = [ctx.enter_context(nc.psum_tensor(f"bank{i}", [P, 512], F32)) for i in range(8)]
        m4, m5, m6, m7 = bank[4:]

        K = sb("K", [P, C_END])
        in_hi = sb("in_hi", [P, KT, SEQ], F32R)
        in_lo = sb("in_lo", [P, KT, SEQ], F32R)
        big = sb("big", [P, KT * SEQ])
        tok = big[:, :].rearrange("p (t d) -> p t d", t=TT_N)
        mixT = big[:, :].rearrange("p (c s) -> p c s", c=KT)
        raw = [sb(f"raw{i}", [P, UNIT]) for i in range(RING)]
        whi = [sb(f"whi{i}", [P, UNIT], F32R) for i in range(RING)]
        wlo = [sb(f"wlo{i}", [P, UNIT], F32R) for i in range(RING)]
        NROW = CONV * 3 * HEADS + KT
        pcol = sb("pcol", [P, NROW + KT + 2])
        wdo_half = sb("wdo_half", [P, 1])
        wao = sb("wao", [P, 1])
        wqk = sb("wqk", [P, 2, P])
        stat = sb("stat", [P, 32])
        mhalf = sb("mhalf", [P, 32])
        ones = sb("ones", [P, P])
        epsr = sb("epsr", [P, 12])
        pcount = sb("pcount", [P, 1])

        mix = ctx.enter_context(ExitStack())

        def mb(name, shape, dt=F32):
            return sb(name, shape, dt, mix)

        sel = mb("sel", [P, HEADS, 28])
        hs = mb("hs", [P, 28])
        cs = mb("cs", [P, 2, TT_N, P // 2])
        qT = mb("qT", [P, SEQ])
        kT = mb("kT", [P, SEQ])
        vT = mb("vT", [P, SEQ])
        zs = mb("zs", [P, SEQ])
        y = mb("y", [P, SEQ])
        th = mb("th", [P, SEQ])
        kh = mb("kh", [P, SEQ])
        T = kh
        kbg = mb("kbg", [P, SEQ])
        kdec = mb("kdec", [P, SEQ])
        vb = mb("vb", [P, SEQ])
        khT = mb("khT", [P, SEQ])
        nwT = khT
        TI = mb("TI", [P, SEQ])
        qsqr = TI
        EGr = TI
        Q = mb("Q", [P, SEQ])
        x0 = Q
        osb = Q
        L = mb("L", [P, SEQ])
        QK = mb("QK", [P, SEQ])
        qd = mb("qd", [P, SEQ])
        S = mb("S", [P, P])
        vn = mb("vn", [P, P])
        dst = mb("dst", [P, 40])
        taps = mb("taps", [P, CONV * 3])
        qkv = mb("qkv", [P, TT_N, 3 * P])
        ra = mb("ra", [P, SEQ])
        sm = ra
        rb = mb("rb", [P, SEQ])
        ex = rb
        aT = mb("aT", [P, 2 * SEQ])
        pT = mb("pT", [P, SEQ])
        oa = pT
        ast = mb("ast", [P, 40])
        junk = mb("junk", [P, SEQ])
        wba_hi = mb("wba_hi", [P, KT * 16], F32R)
        wba_lo = mb("wba_lo", [P, KT * 16], F32R)
        wba = y[:, 0:KT * 16]
        prow = th[0:CONV * 24 + KT, 0:P]
        prow2 = th[0:KT + 2, P:2 * P]
        posi = mb("posi", [P, TT_N], I32)
        gt = kbg[:, :].rearrange("p (n c) -> p n c", c=32)
        hb = mb("hb", [P, 2 * HEADS])

        def four(t, w=P):
            return t.rearrange("p (t d) -> p t d", t=TT_N)

        def per_tile(ap4, w=P):
            return ap4.unsqueeze(2).broadcast_to([P, TT_N, w])

        def each_tile(ap, w=P):
            return ap.unsqueeze(1).broadcast_to([P, TT_N, w])

        def const(o, n=P):
            return K[:, o:o + n]

        def gate(kind):
            return hs[:, kind * 4:kind * 4 + 4]

        ident = const(C_ID)
        conv_tap = lambda tap, c: pcol[:, tap * 24 + c:tap * 24 + c + 1]

        small_in = sem("small_in"); x_in = [sem(f"x_in{t}") for t in range(TT_N)]
        raw_in = [sem(f"raw_in{i}") for i in range(RING)]
        hi_made = sem("hi_made"); lo_made = sem("lo_made"); unit_used = sem("unit_used")
        consts_in = sem("consts_in"); pool_set = sem("pool_set")
        rows_ps = sem("rows_ps"); cols_made = sem("cols_made")
        sumsq = sem("sumsq"); rstd = sem("rstd"); scaled = sem("scaled"); turned = sem("turned")
        in_hi_made = sem("in_hi_made"); in_lo_made = sem("in_lo_made")
        ba_split = sem("ba_split"); ba_ps = sem("ba_ps"); act0 = sem("act0"); dve0 = sem("dve0"); cum_ps = sem("cum_ps")
        gates_ready = sem("gates_ready")
        proj_ps = sem("proj_ps"); conv_done = sem("conv_done"); tanh_done = sem("tanh_done"); dproj = sem("dproj")
        hs_ready = sem("hs_ready"); qsq = sem("qsq"); d_in_ps = sem("d_in_ps"); kss = sem("kss"); qss = sem("qss")
        rn_ready = sem("rn_ready"); vb_ready = sem("vb_ready"); x_ready = sem("x_ready"); decay = sem("decay")
        kh_ready = sem("kh_ready"); pool_d = sem("pool_d"); khT_ps = sem("khT_ps"); khT_ready = sem("khT_ready")
        kk_ps = sem("kk_ps"); L_ready = sem("L_ready"); ti_ps = sem("ti_ps"); ti_ready = sem("ti_ready")
        q_ps = sem("q_ps"); q_made = sem("q_made"); u_ps = sem("u_ps"); lvl = sem("lvl")
        wT_ps = sem("wT_ps"); wT_ready = sem("wT_ready"); vn_ps = sem("vn_ps"); vn_ready = sem("vn_ready")
        S_ps = sem("S_ps"); S_ready = sem("S_ready"); o_ps = sem("o_ps"); o_ready = sem("o_ready"); oss = sem("oss")
        on_ready = sem("on_ready"); oT_ps = sem("oT_ps"); mix_done = sem("mix_done")
        a_ps = sem("a_ps"); qkv_ready = sem("qkv_ready"); a_sq = sem("a_sq"); a_ss = sem("a_ss"); pool_a = sem("pool_a")
        qk_ready = sem("qk_ready"); aT_ps = sem("aT_ps"); aT_ready = sem("aT_ready"); s_ps = sem("s_ps")
        s_max = sem("s_max"); sm_ready = sem("sm_ready"); ex_ready = sem("ex_ready"); p_ready = sem("p_ready"); rden = sem("rden")
        pT_ps = sem("pT_ps"); pT_ready = sem("pT_ready"); pv_ps = sem("pv_ps"); oa_ready = sem("oa_ready")
        oass = sem("oass"); oan_ready = sem("oan_ready"); oaT_ps = sem("oaT_ps"); amix = sem("amix")
        mhi = sem("mhi"); mlo = sem("mlo"); xr_in = sem("xr_in"); out_ps = sem("out_ps"); res = sem("res")
        ss2 = sem("ss2"); rstd2 = sem("rstd2"); h2 = sem("h2"); turned2 = sem("turned2")
        h2hi = sem("h2hi"); h2lo = sem("h2lo")
        gu_ps = sem("gu_ps"); silu_done = sem("silu_done"); prod = sem("prod"); acthi = sem("acthi"); actlo = sem("actlo")
        dn_ps = sem("dn_ps"); stored = sem("stored")

        mix.close()
        act_hi = sb("act_hi", [P, FPG, SEQ], F32R)
        act_lo = sb("act_lo", [P, FPG, SEQ], F32R)
        gs = sb("gs", [P, SEQ])
        pr = sb("pr", [P, SEQ])
        h2c = sb("h2c", [P, 4, SEQ])

        x_t = x[0].rearrange("(t p) d -> p t d", p=P)
        out_t = out[0].rearrange("(t p) d -> p t d", p=P)
        win = w_in[0].rearrange("(k p) n -> p k n", p=P)
        wo = w_out[0].rearrange("(k p) n -> p k n", p=P)
        wgu = w_gate_up[0].rearrange("(k p) n -> p k n", p=P)
        wdn = w_down[0].rearrange("(k p) n -> p k n", p=P)
        A0 = 4 * GW + 2 * HEADS


        def value(e, v):
            return v if isinstance(v, int) else e.snap(v)

        def split_wait(u0, c):
            return 4 * u0 + 16 * (c // RING + 1)

        def hi_part(e, u0, c, n=UNIT):
            e.wait_ge(raw_in[c % RING], split_wait(u0, c))
            if not (isinstance(u0, int) and u0 + c < RING):
                e.wait_ge(unit_used, u0 + c - RING + 1)
            e.activation(whi[c % RING][:, 0:n], raw[c % RING][:, 0:n], ACT.Copy).then_inc(hi_made, 1)

        def lo_part(e, u0, c, n=UNIT):
            e.wait_ge(hi_made, u0 + c + 1)
            e.tensor_tensor(wlo[c % RING][:, 0:n], raw[c % RING][:, 0:n], whi[c % RING][:, 0:n],
                            ALU.subtract).then_inc(lo_made, 1)

        def ahead(part, e, u0, c, last=False):
            c += AHEAD
            part(e, u0, c, A_N if c < A_UNITS or (c >= H_UNITS and not last) else UNIT)

        def run(stages, names, skip):
            for name in names:
                if name in stages and not (skip and name[0] in "dquvr") and not (skip and name in ("a_sq", "a_tail")):
                    stages[name]()

        block = ctx.enter_context(nc.Block())

        @block.sync
        def _(sp):
            for t in range(TT_N):
                sp.dma_start(tok[:, t], x_t[:, t]).then_inc(x_in[t], 16)

            def load(u0, c, dst, src):
                if not (isinstance(u0, int) and u0 + c < RING):
                    split = value(sp, u0 + c - RING + 1 + (c == A_UNITS - 1))
                    sp.wait_ge(raw_in[c % RING], 16)
                    sp.wait_ge(lo_made, split)
                sp.dma_start(dst, src).then_inc(raw_in[c % RING], 16)

            def head(h):
                u0 = h * H_UNITS
                for k in range(A_UNITS):
                    src = win[:, k, A0:A0 + 3 * GW].rearrange("p (c n) -> p c n", c=3)[:, :, bass.ds(h * P, P)]
                    load(u0, k, raw[k % RING][:, 0:A_N].rearrange("p (c n) -> p c n", c=3), src)
                for j in range(D_UNITS):
                    c, q = j // 4, j % 4
                    src = win[:, D_KT * q:D_KT * (q + 1), bass.ds(h * P + c * GW, P)]
                    load(u0, A_UNITS + j, raw[j % RING][:, :].rearrange("p (k n) -> p k n", k=D_KT), src)

            head(0)
            with sp.Fori(1, HEADS) as h:
                head(h)
            for c in range(4):
                for k in range(KT):
                    load(U_OUT, c * KT + k, raw[k % RING][:, :], wo[:, k, c * 512:(c + 1) * 512])
            with sp.Fori(0, FG) as g:
                with sp.Fori(0, FPG) as f:
                    u0 = U_FFN + g * F_UNITS + f * GU_UNITS
                    for j in range(GU_UNITS):
                        c, q = j // 4, j % 4
                        src = wgu[:, D_KT * q:D_KT * (q + 1), bass.ds((g * FPG + f) * P + c * FF, P)]
                        load(u0, j, raw[j % RING][:, :].rearrange("p (k n) -> p k n", k=D_KT), src)
                u0 = U_FFN + g * F_UNITS + FPG * GU_UNITS
                for j in range(DN_UNITS):
                    c, k = j // FPG, j % FPG
                    src = wdn[:, bass.ds(g * FPG + k, 1), c * 512:(c + 1) * 512]
                    load(u0, j, raw[j % RING][:, :].rearrange("p (k n) -> p k n", k=1), src)
            for c in range(4):
                for t in range(TT_N):
                    sp.wait_ge(res, FG * 16 + 4 * c + t + 1)
                    sp.dma_start(out_t[:, t, c * 512:(c + 1) * 512],
                                 tok[:, t, c * 512:(c + 1) * 512]).then_inc(stored, 16)
            sp.wait_ge(stored, 16 * 16)

        @block.tensor
        def _(pe):
            def turn(dst_, src_):
                return pe.transpose(dst_, src_, ident)

            def tiles(dst_, lhs, rhs, done):
                for t in range(TT_N):
                    o = pe.matmul(dst_[:, t * P:(t + 1) * P], lhs[:, t * P:(t + 1) * P], rhs[:, t * P:(t + 1) * P],
                                  start=True, stop=True)
                o.then_inc(done, 1)

            def turns(dst_, src_, done):
                for t in range(TT_N):
                    o = turn(dst_[:, t * P:(t + 1) * P], src_[:, t * P:(t + 1) * P])
                o.then_inc(done, 1)

            pe.wait_ge(consts_in, 16)
            pe.wait_ge(small_in, 16 * SMALL)
            pe.transpose(bank[0][:, 0:NROW], prow, ident[0:NROW, 0:NROW]).then_inc(rows_ps, 1)
            pe.transpose(bank[1][:, 0:KT + 2], prow2, ident[0:KT + 2, 0:KT + 2]).then_inc(rows_ps, 1)
            for k in range(KT):
                if k == 0:
                    pe.wait_ge(cols_made, 3)
                    pe.wait_ge(scaled, TT_N)
                if k >= 8:
                    pe.wait_ge(in_lo_made, k - 7)
                for t in range(TT_N):
                    o = turn(bank[k % 8][:, t * P:(t + 1) * P], tok[:, t, k * P:(k + 1) * P])
                o.then_inc(turned, 1)
            pe.wait_ge(in_lo_made, KT)
            pe.wait_ge(ba_split, 2)
            for t in range(TT_N):
                for k in range(KT):
                    for n, (a, b) in enumerate(((in_hi, wba_hi), (in_hi, wba_lo), (in_lo, wba_hi))):
                        o = pe.matmul(bank[0][:, t * 16:(t + 1) * 16], a[:, k, t * P:(t + 1) * P],
                                      b[:, k * 16:(k + 1) * 16], start=(k == 0 and n == 0),
                                      stop=(k == KT - 1 and n == 2))
            o.then_inc(ba_ps, 1)
            pe.wait_ge(dve0, DVE_G)
            pe.wait_ge(pool_set, 5)
            pe.matmul(bank[1][:, 0:32], const(C_U), gt[:, 9], start=True, stop=True)
            pe.matmul(bank[1][:, 32:64], ones[:, :], gt[:, 9], start=True, stop=True).then_inc(cum_ps, 1)
            pe.wait_ge(gates_ready, 1)

            def split3(dst_, pairs, start, stop):
                for n, (a, b) in enumerate(pairs):
                    o = pe.matmul(dst_, a, b, start=(start and n == 0), stop=(stop and n == 2))
                return o

            def body(h, first, last):
                d = h - 1
                st = stages(h, d, first)
                u0 = h * H_UNITS
                for k in range(A_UNITS):
                    pe.wait_ge(lo_made, u0 + k + 1)
                    for t in range(TT_N):
                        if k == 0 and not first:
                            (lambda: pe.wait_ge(dproj, 17 * d + 15), lambda: pe.wait_ge(dproj, 17 * d + 17),
                             lambda: pe.wait_ge(sm_ready, 4 * d + 4), lambda: pe.wait_ge(oa_ready, d + 1))[t]()
                        c = slice(t * P, (t + 1) * P)
                        hi, lo = whi[k % RING][:, 0:A_N], wlo[k % RING][:, 0:A_N]
                        o = split3(bank[t][:, 0:A_N], ((in_hi[:, k, c], hi), (in_hi[:, k, c], lo), (in_lo[:, k, c], hi)),
                                   k == 0, k == KT - 1)
                        if t == TT_N - 1:
                            o.then_inc(unit_used, 1)
                        elif k == KT - 1:
                            o.then_inc(a_ps, 1)
                    run(st, A_STAGES.get(k, []), first)
                for j in range(D_UNITS):
                    c, q = j // 4, j % 4
                    pe.wait_ge(lo_made, u0 + A_UNITS + j + 1)
                    if q == 0:
                        if c < 2:
                            pe.wait_ge(qkv_ready, 4 * h + c + 1)
                        else:
                            pe.wait_ge(dproj, 17 * h + 5 * (c - 2) + 5)
                    for kk in range(D_KT):
                        k, w = D_KT * q + kk, slice(kk * P, (kk + 1) * P)
                        hi, lo = whi[j % RING][:, w], wlo[j % RING][:, w]
                        o = split3(bank[c % 2][:, :], ((hi, in_hi[:, k]), (hi, in_lo[:, k]), (lo, in_hi[:, k])),
                                   k == 0, k == KT - 1)
                    o.then_inc(unit_used, 1)
                    run(st, D_STAGES.get(j, []), first)

            def stages(h, d, first):
                def d_tokens():
                    pe.wait_ge(dproj, 17 * d + 17)
                    turns(m4, kT, d_in_ps)
                    pe.wait_ge(pT_ready, 4 * d + 4)
                    turns(m5, vT, d_in_ps)
                    pe.wait_ge(hs_ready, d + 1)
                    for t in range(TT_N):
                        g = hs[:, G_ * 4 + t:G_ * 4 + t + 1].broadcast_to([P, P])
                        o = pe.matmul(m6[:, t * P:(t + 1) * P], g, const(C_U), start=True, stop=True)
                    o.then_inc(d_in_ps, 1)
                    pe.wait_ge(qsq, d + 1)
                    for t in range(TT_N):
                        o = pe.matmul(m7[:, t:t + 1], qsqr[:, t * P:(t + 1) * P], pcount[:, :], start=True, stop=True)
                    o.then_inc(d_in_ps, 1)

                def d_khat():
                    pe.wait_ge(kh_ready, d + 1)
                    turns(m4, kh, khT_ps)

                def d_kk():
                    pe.wait_ge(khT_ready, d + 1)
                    pe.wait_ge(vb_ready, d + 1)
                    tiles(m5, khT, khT, kk_ps)
                    pe.wait_ge(decay, 3 * d + 3)
                    tiles(m6, khT, qT, kk_ps)

                def d_ti():
                    pe.wait_ge(pool_d, 13 * d + 10)
                    turns(m4, T, ti_ps)

                def level_q(i):
                    if i == 0:
                        pe.wait_ge(ti_ready, d + 1)
                        pe.wait_ge(L_ready, 2 * d + 2)
                    else:
                        pe.wait_ge(lvl, 11 * d + 2 * i)
                    tiles(m5, L, TI, q_ps)

                def level_u(i):
                    pe.wait_ge(q_made, NL * d + i + 1)
                    tiles(m6, T, Q, u_ps)
                    if i < NL - 1:
                        if i == 0:
                            pe.wait_ge(amix, d + 1)
                        tiles(m7, Q, T, u_ps)

                def d_wt():
                    pe.wait_ge(lvl, 11 * d + 11)
                    pe.wait_ge(pool_d, 13 * d + 8)
                    tiles(m5, kbg, TI, wT_ps)

                def new_values(t):
                    c = slice(t * P, (t + 1) * P)
                    if t:
                        pe.wait_ge(wT_ready, d + 1)
                        pe.wait_ge(S_ready, 3 * d + t)
                    o = pe.matmul(m6[:, 0:P], TI[:, c], vb[:, c], start=True, stop=(t == 0))
                    if t:
                        o = pe.matmul(m6[:, 0:P], nwT[:, c], S[:, :], start=False, stop=True)
                    o.then_inc(vn_ps, 1)

                def outputs(t):
                    c = slice(t * P, (t + 1) * P)
                    pe.wait_ge(vn_ready, 4 * d + t + 1)
                    if t:
                        pe.matmul(m7[:, c], qd[:, c], S[:, :], start=True, stop=False)
                    o = pe.matmul(m7[:, c], QK[:, c], vn[:, :], start=(t == 0), stop=True)
                    if t < TT_N - 1:
                        pe.matmul(m4[:, 0:P], kdec[:, c], vn[:, :], start=True, stop=True).then_inc(S_ps, 1)
                    else:
                        o.then_inc(o_ps, 1)

                def d_turn():
                    pe.wait_ge(pool_d, 13 * d + 13)
                    turns(m4, osb, oT_ps)

                def a_tail():
                    pe.wait_ge(pool_a, 18 * d + 18)
                    pe.wait_ge(qss, d + 1)
                    turns(m7, oa, oaT_ps)

                def a_turn():
                    for c, b in ((0, 2), (1, 3)):
                        pe.wait_ge(pool_a, 18 * h + 9 + 6 * c)
                        pe.wait_ge(qkv_ready, 4 * h + 3 + c)
                        for t in range(TT_N):
                            o = turn(bank[b][:, t * P:(t + 1) * P], qkv[:, t, c * P:(c + 1) * P])
                        o.then_inc(aT_ps, 1)

                def a_score(t):
                    pe.wait_ge(aT_ready, 2 * h + 2)
                    if t:
                        pe.wait_ge(sm_ready, 4 * h + t)
                    pe.matmul(bank[2][:, 0:(t + 1) * P], aT[:, t * P:(t + 1) * P], aT[:, SEQ:SEQ + (t + 1) * P],
                              start=True, stop=True).then_inc(s_ps, 1)

                def a_prob(t):
                    pe.wait_ge(p_ready, 4 * h + t + 1)
                    if t:
                        pe.wait_ge(pT_ready, 4 * h + t)
                    elif not first:
                        pe.wait_ge(wT_ready, d + 1)
                    for j in range(t + 1):
                        o = turn(m5[:, j * P:(j + 1) * P], ex[:, j * P:(j + 1) * P])
                    o.then_inc(pT_ps, 1)

                def a_pv(t):
                    pe.wait_ge(pT_ready, 4 * h + t + 1)
                    for j in range(t + 1):
                        o = pe.matmul(bank[3][:, t * P:(t + 1) * P], pT[:, j * P:(j + 1) * P],
                                      qkv[:, j, 2 * P:3 * P], start=(j == 0), stop=(j == t))
                    o.then_inc(pv_ps, 1)

                st = dict(d_tokens=d_tokens, d_khat=d_khat, d_kk=d_kk, d_ti=d_ti, d_wt=d_wt, d_turn=d_turn,
                          a_tail=a_tail, a_turn=a_turn)
                for i in range(NL):
                    st[f"q{i}"] = lambda i=i: level_q(i)
                    st[f"u{i}"] = lambda i=i: level_u(i)
                for t in range(TT_N):
                    st[f"v{t}"] = lambda t=t: new_values(t)
                    st[f"r{t}"] = lambda t=t: outputs(t)
                    st[f"a_score{t}"] = lambda t=t: a_score(t)
                    st[f"a_prob{t}"] = lambda t=t: a_prob(t)
                    st[f"a_pv{t}"] = lambda t=t: a_pv(t)
                return st

            body(0, True, False)
            with pe.Fori(1, HEADS - 1) as h:
                body(h, False, False)
            body(HEADS - 1, False, True)
            st = stages(HEADS, HEADS - 1, False)
            for names in list(A_STAGES.values()) + list(D_STAGES.values()):
                run(st, [n for n in names if n[0] in "dquvr" or n in ("a_sq", "a_tail")], False)

            for c in range(4):
                for k in range(KT):
                    u = c * KT + k
                    pe.wait_ge(lo_made, U_OUT + u + 1)
                    if c == 0:
                        pe.wait_ge(mlo, k + 1)
                    for t in range(TT_N):
                        if c >= 2 and k == 0:
                            pe.wait_ge(res, 4 * (c - 2) + t + 1)
                        s_ = slice(t * P, (t + 1) * P)
                        hi, lo = whi[u % RING][:, :], wlo[u % RING][:, :]
                        o = split3(bank[4 * (c % 2) + t][:, :],
                                   ((in_hi[:, k, s_], hi), (in_hi[:, k, s_], lo), (in_lo[:, k, s_], hi)),
                                   k == 0, k == KT - 1)
                        if t == TT_N - 1:
                            o.then_inc(unit_used, 1)
                        elif k == KT - 1:
                            o.then_inc(out_ps, 1)
            for k in range(KT):
                pe.wait_ge(h2, k + 1)
                if k >= 8:
                    pe.wait_ge(h2lo, k - 7)
                for t in range(TT_N):
                    o = turn(bank[k % 8][:, t * P:(t + 1) * P], h2c[:, k % 4, t * P:(t + 1) * P])
                o.then_inc(turned2, 1)
            pe.wait_ge(h2lo, KT)

            def ffn_group(g):
                with pe.Fori(0, FPG) as f:
                    u0 = U_FFN + g * F_UNITS + f * GU_UNITS
                    F = g * FPG + f
                    pe.wait_ge(res, 16 + 16 * g)
                    for j in range(GU_UNITS):
                        c, q = j // 4, j % 4
                        pe.wait_ge(lo_made, u0 + j + 1)
                        for kk in range(D_KT):
                            k, w = D_KT * q + kk, slice(kk * P, (kk + 1) * P)
                            hi, lo = whi[j % RING][:, w], wlo[j % RING][:, w]
                            o = split3(bank[c][:, :], ((hi, in_hi[:, k]), (hi, in_lo[:, k]), (lo, in_hi[:, k])),
                                       k == 0, k == KT - 1)
                        o.then_inc(unit_used, 1)
                u0 = U_FFN + g * F_UNITS + FPG * GU_UNITS
                for c in range(4):
                    for k in range(FPG):
                        j = c * FPG + k
                        pe.wait_ge(lo_made, u0 + j + 1)
                        if c == 0:
                            pe.wait_ge(actlo, g * FPG + k + 1)
                        for t in range(TT_N):
                            if k == 0 and c >= 2:
                                pe.wait_ge(res, 16 + 16 * g + 4 * (c - 2) + t + 1)
                            s_ = slice(t * P, (t + 1) * P)
                            hi, lo = whi[j % RING][:, :], wlo[j % RING][:, :]
                            o = split3(bank[4 * ((c + 1) % 2) + t][:, :],
                                       ((act_hi[:, k, s_], hi), (act_hi[:, k, s_], lo), (act_lo[:, k, s_], hi)),
                                       k == 0, k == FPG - 1)
                            if t == TT_N - 1:
                                o.then_inc(unit_used, 1)
                            elif k == FPG - 1:
                                o.then_inc(dn_ps, 1)

            with pe.Fori(0, FG) as g:
                ffn_group(g)

        @block.scalar
        def _(act):
            for dst_, src_ in ((prow[0:CONV * 24], conv_w[0].rearrange("t (c n) -> (t c) n", n=P)),
                               (prow[CONV * 24:NROW], attn_norm_w[0].rearrange("(c n) -> c n", n=P)),
                               (prow2[0:KT], ffn_norm_w[0].rearrange("(c n) -> c n", n=P)),
                               (prow2[KT:KT + 1], delta_out_norm_w), (prow2[KT + 1:KT + 2], attn_out_norm_w)):
                act.dma_start(dst_, src_).then_inc(small_in, 16)
            act.dma_start(K[:, :], cst).then_inc(consts_in, 16)
            act.dma_start(wba.rearrange("p (k n) -> p k n", k=KT), win[:, :, 4 * GW:A0]).then_inc(small_in, 16)
            for dst_, src_ in ((wqk[:, 0, :], q_norm_w), (wqk[:, 1, :], k_norm_w), (hb[:, 0:HEADS], a_log),
                               (hb[:, HEADS:], dt_bias)):
                act.dma_start(dst_, src_.broadcast_to([P, dst_.shape[-1]])).then_inc(small_in, 16)
            act.dma_start(posi[:, :], positions[0].rearrange("(t p) -> p t", p=P),
                          allow_slow_non_contiguous=True).then_inc(small_in, 16)

            for t in range(TT_N):
                act.wait_ge(x_in[t], 16)
                act.activation(in_lo[:, 4 * t:4 * t + 4, :], tok[:, t].rearrange("p (a b) -> p a b", a=4), ACT.Square,
                               accum_out=stat[:, t:t + 1]).then_inc(sumsq, 1)
            act.wait_ge(small_in, 16 * SMALL)
            act.activation(wba_hi[:, :], wba, ACT.Copy).then_inc(ba_split, 1)
            act.wait_ge(dve0, DVE_SIN)
            act.activation(cs[:, 1].rearrange("p t n -> p (t n)"), aT[:, 0:256], ACT.Sin).then_inc(act0, 1)
            act.activation(cs[:, 0].rearrange("p t n -> p (t n)"), aT[:, 256:512], ACT.Sin).then_inc(act0, 1)
            act.wait_ge(cols_made, 3)
            for k in range(KT):
                act.wait_ge(turned, k + 1)
                act.activation(in_hi[:, k], bank[k % 8][:, :], ACT.Copy,
                               scale=pcol[:, CONV * 24 + k:CONV * 24 + k + 1]).then_inc(in_hi_made, 1)
            for u in range(AHEAD):
                hi_part(act, 0, u, A_N)
            act.wait_ge(dve0, DVE_DB)
            act.activation(gt[:, 2], gt[:, 0], ACT.Tanh, scale=0.5).then_inc(act0, 1)
            act.wait_ge(dve0, DVE_ABS)
            act.activation(gt[:, 6], gt[:, 5], ACT.Exp, scale=-1.0).then_inc(act0, 1)
            act.wait_ge(act0, 4)
            act.activation(gt[:, 7], gt[:, 6], ACT.Ln, bias=1.0).then_inc(act0, 1)
            act.activation(ast[:, 0:HEADS], hb[:, 0:HEADS], ACT.Exp).then_inc(act0, 1)
            act.wait_ge(dve0, DVE_EXPS)
            act.activation(gt[:, 13], gt[:, 10], ACT.Exp).then_inc(act0, 1)
            act.activation(gt[:, 14], gt[:, 12], ACT.Exp).then_inc(act0, 1)
            act.activation(gt[:, 15], gt[:, 11], ACT.Exp).then_inc(act0, 1)

            def body(h, first, last):
                u0 = h * H_UNITS
                st = stages(h, h - 1, u0, first)
                for c in range(H_UNITS):
                    ahead(hi_part, act, u0, c, last)
                    run(st, (A_STAGES.get(c, []) if c < A_UNITS else D_STAGES.get(c - A_UNITS, [])), first)

            def stages(h, d, u0, first):
                def d_tokens():
                    act.wait_ge(dproj, 17 * d + 17)
                    act.activation(qsqr[:, :], qT[:, :], ACT.Square).then_inc(qsq, 1)
                    act.wait_ge(d_in_ps, 4 * d + 1)
                    for t in range(TT_N):
                        c = slice(t * P, (t + 1) * P)
                        act.activation(junk[:, c], m4[:, c], ACT.Square, accum_out=dst[:, t:t + 1]).then_inc(kss, 1)
                    act.wait_ge(x_ready, 3 * d + 2)
                    act.activation(L[:, :], L[:, :], ACT.Exp, scale=-1.0).then_inc(decay, 1)
                    act.wait_ge(x_ready, 3 * d + 3)
                    act.activation(QK[:, :], QK[:, :], ACT.Exp).then_inc(decay, 1)
                    act.wait_ge(d_in_ps, 4 * d + 4)
                    act.activation(EGr[:, :], m6[:, :], ACT.Exp).then_inc(decay, 1)

                def a_sq():
                    act.wait_ge(kss, 4 * d + 4)
                    act.wait_ge(oa_ready, d + 1)
                    for t in range(TT_N):
                        c = slice(t * P, (t + 1) * P)
                        act.activation(junk[:, c], oa[:, c], ACT.Square, accum_out=ast[:, t:t + 1]).then_inc(oass, 1)

                def d_khat():
                    act.wait_ge(khT_ps, d + 1)
                    act.activation(khT[:, :], m4[:, :], ACT.Copy).then_inc(khT_ready, 1)

                def d_ti():
                    act.wait_ge(pool_d, 13 * d + 8)
                    act.wait_ge(ti_ps, d + 1)
                    act.activation(TI[:, :], m4[:, :], ACT.Copy).then_inc(ti_ready, 1)

                def d_wt():
                    act.wait_ge(wT_ps, d + 1)
                    act.activation(nwT[:, :], m5[:, :], ACT.Copy, scale=-1.0).then_inc(wT_ready, 1)

                def d_norm():
                    act.wait_ge(oass, 4 * d + 4)
                    act.wait_ge(o_ready, d + 1)
                    for t in range(TT_N):
                        c = slice(t * P, (t + 1) * P)
                        act.activation(junk[:, c], osb[:, c], ACT.Square,
                                       accum_out=dst[:, 24 + t:25 + t]).then_inc(oss, 1)

                def a_evac():
                    if not first:
                        act.wait_ge(pv_ps, 4 * h)
                    for t in range(TT_N):
                        if t < TT_N - 1:
                            act.wait_ge(a_ps, 3 * h + t + 1)
                        else:
                            act.wait_ge(unit_used, u0 + A_UNITS)
                        act.activation(qkv[:, t, :], bank[t][:, 0:A_N], ACT.Copy).then_inc(qkv_ready, 1)

                def conv(c):
                    if c < 3:
                        act.wait_ge(dproj, 17 * h + 5 + 5 * c)
                        act.activation(th[:, :], y[:, :], ACT.Tanh).then_inc(tanh_done, 1)
                    else:
                        act.wait_ge(dproj, 17 * h + 16)
                        act.wait_ge(unit_used, u0 + H_UNITS)
                        act.activation(th[:, :], bank[1][:, :], ACT.Tanh, scale=0.5).then_inc(tanh_done, 1)

                def a_turn():
                    for c in range(2):
                        act.wait_ge(aT_ps, 2 * h + c + 1)
                        act.activation(aT[:, c * SEQ:(c + 1) * SEQ], bank[2 + c][:, :], ACT.Copy).then_inc(aT_ready, 1)

                def a_score(t):
                    n = (t + 1) * P
                    act.wait_ge(sm_ready, 4 * h + t + 1)
                    if t:
                        act.wait_ge(pT_ps, 4 * h + t)
                    act.activation(ex[:, 0:n], sm[:, 0:n], ACT.Exp, scale=SCALE,
                                   bias=ast[:, 28 + t:29 + t]).then_inc(ex_ready, 1)

                def a_prob(t):
                    n = (t + 1) * P
                    act.wait_ge(pT_ps, 4 * h + t + 1)
                    if t:
                        act.wait_ge(pv_ps, 4 * h + t)
                    elif not first:
                        act.wait_ge(oaT_ps, h)
                    act.activation(pT[:, 0:n], m5[:, 0:n], ACT.Copy).then_inc(pT_ready, 1)

                st = dict(d_tokens=d_tokens, a_sq=a_sq, d_khat=d_khat, d_ti=d_ti, d_wt=d_wt, d_norm=d_norm,
                          a_evac=a_evac, a_turn=a_turn)
                for c in range(4):
                    st[f"conv{c}"] = lambda c=c: conv(c)
                    st[f"a_score{c}"] = lambda c=c: a_score(c)
                    st[f"a_prob{c}"] = lambda c=c: a_prob(c)
                return st

            body(0, True, False)
            with act.Fori(1, HEADS - 1) as h:
                body(h, False, False)
            body(HEADS - 1, False, True)
            st = stages(HEADS, HEADS - 1, None, False)
            for names in list(A_STAGES.values()) + list(D_STAGES.values()):
                run(st, [n for n in names if n[0] in "dquvr" or n in ("a_sq", "a_tail")], False)

            act.wait_ge(unit_used, U_OUT)
            act.wait_ge(amix, HEADS)
            act.wait_ge(mix_done, HEADS)
            for k in range(KT):
                act.activation(in_hi[:, k], mixT[:, k], ACT.Copy).then_inc(mhi, 1)
            act.wait_ge(mlo, KT)
            for t in range(TT_N):
                act.dma_start(tok[:, t], x_t[:, t]).then_inc(xr_in, 16)
            for c in range(4):
                for k in range(KT):
                    hi_part(act, U_OUT, c * KT + k + AHEAD)
                for t in range(TT_N):
                    act.wait_ge(res, 4 * c + t + 1)
                    act.activation(gs[:, :], tok[:, t, c * 512:(c + 1) * 512], ACT.Square,
                                   accum_out=stat[:, 4 * t + c:4 * t + c + 1]).then_inc(ss2, 1)
                    act.wait_ge(ss2, 4 * c + t + 1)
            for k in range(KT):
                act.wait_ge(turned2, k + 1)
                act.activation(in_hi[:, k], bank[k % 8][:, :], ACT.Copy,
                               scale=pcol[:, NROW + k:NROW + k + 1]).then_inc(h2hi, 1)

            def ffn_group(g, last):
                with act.Fori(0, FPG) as f:
                    u0 = U_FFN + g * F_UNITS + f * GU_UNITS
                    F = g * FPG + f
                    for j in range(GU_UNITS):
                        hi_part(act, u0, j + AHEAD)
                        if j == 3:
                            act.wait_ge(unit_used, u0 + 4)
                            act.activation(gs[:, :], bank[0][:, :], ACT.Silu).then_inc(silu_done, 1)
                    act.wait_ge(prod, F + 1)
                    act.activation(act_hi[:, bass.ds(f, 1), :], pr[:, :].unsqueeze(1), ACT.Copy).then_inc(acthi, 1)
                u0 = U_FFN + g * F_UNITS + FPG * GU_UNITS
                for j in range(DN_UNITS - AHEAD * last):
                    hi_part(act, u0, j + AHEAD)

            with act.Fori(0, FG - 1) as g:
                ffn_group(g, False)
            ffn_group(FG - 1, True)

        @block.vector
        def _(dve):
            def step(ins, done, value):
                ins.then_inc(done, 1)
                dve.wait_ge(done, value)

            n0 = [0]

            def start(ins):
                n0[0] += 1
                step(ins, dve0, n0[0])

            dve.wait_ge(consts_in, 16)
            dve.wait_ge(small_in, 16 * SMALL)
            A, B, C, D = (aT[:, i * 256:(i + 1) * 256] for i in (0, 1, 2, 3))
            a3 = A.rearrange("p (t n) -> p t n", t=TT_N)
            MAGIC = 1.5 * 2.0 ** 23
            two_pi = 2 * np.pi
            c1 = round(two_pi * 2 ** 9) / 2 ** 9
            c2 = round((two_pi - c1) * 2 ** 27) / 2 ** 27
            c3 = two_pi - c1 - c2
            pi_in = 3.1415925
            start(dve.tensor_copy(ast[:, 36:40], posi[:, :]))
            start(dve.tensor_tensor(a3, per_tile(ast[:, 36:40], P // 2), each_tile(K[:, C_FREQ:C_END], P // 2), ALU.mult))
            start(dve.tensor_scalar(B, A, float(1 / two_pi), MAGIC, ALU.mult, ALU.add))
            start(dve.tensor_scalar(B, B, MAGIC, None, ALU.subtract))
            start(dve.tensor_scalar(C, B, 2.0 ** -11, MAGIC, ALU.mult, ALU.add))
            start(dve.tensor_scalar(C, C, MAGIC, 2.0 ** 11, ALU.subtract, ALU.mult))
            start(dve.tensor_tensor(D, B, C, ALU.subtract))
            for turns_, part in ((C, c1), (D, c1), (C, c2), (D, c2), (B, c3)):
                start(dve.scalar_tensor_tensor(A, turns_, -float(part), A, ALU.mult, ALU.add))
            start(dve.tensor_scalar(A, A, -pi_in, pi_in, ALU.max, ALU.min))
            start(dve.tensor_scalar(B, A, float(np.pi / 2), None, ALU.add))
            start(dve.tensor_scalar(C, B, float(np.pi), -float(two_pi), ALU.is_gt, ALU.mult))
            start(dve.tensor_tensor(B, B, C, ALU.add))
            start(dve.tensor_scalar(B, B, -pi_in, pi_in, ALU.max, ALU.min))
            assert n0[0] == DVE_SIN
            dve.wait_ge(rows_ps, 1)
            dve.tensor_scalar(pcol[:, 0:96], bank[0][:, 0:96], 0.5, None, ALU.mult).then_inc(cols_made, 1)
            dve.tensor_copy(pcol[:, 96:NROW], bank[0][:, 96:NROW]).then_inc(cols_made, 1)
            dve.wait_ge(rows_ps, 2)
            step(dve.tensor_copy(pcol[:, NROW:], bank[1][:, 0:KT + 2]), cols_made, 3)
            root = float(P) ** 0.5
            dve.tensor_scalar(wdo_half[:, :], pcol[:, NROW + KT:NROW + KT + 1], 0.5 * root, None,
                              ALU.mult).then_inc(cols_made, 1)
            dve.tensor_scalar(wao[:, :], pcol[:, NROW + KT + 1:NROW + KT + 2], root, None, ALU.mult).then_inc(cols_made, 1)
            dve.tensor_scalar(wqk[:, :, :], wqk[:, :, :], root, None, ALU.mult).then_inc(cols_made, 1)
            dve.wait_ge(ba_split, 1)
            dve.tensor_tensor(wba_lo[:, :], wba, wba_hi[:, :], ALU.subtract).then_inc(ba_split, 1)
            for t in range(TT_N):
                dve.wait_ge(rstd, t + 1)
                dve.tensor_scalar(tok[:, t], tok[:, t], stat[:, 8 + t:9 + t], None, ALU.mult).then_inc(scaled, 1)
            for k in range(KT):
                dve.wait_ge(in_hi_made, k + 1)
                dve.scalar_tensor_tensor(in_lo[:, k], bank[k % 8][:, :], pcol[:, 96 + k:97 + k], in_hi[:, k],
                                         ALU.mult, ALU.subtract).then_inc(in_lo_made, 1)
            for u in range(AHEAD):
                lo_part(dve, 0, u, A_N)
            ba = bank[0][:, 0:64].rearrange("p (t n) -> p t n", t=TT_N)

            def th_(i):
                return gt[:, i].rearrange("p (t n) -> p t n", t=TT_N)

            dve.wait_ge(ba_ps, 1)
            start(dve.tensor_copy(th_(0), ba[:, :, 0:HEADS]))
            start(dve.tensor_tensor(th_(1), ba[:, :, HEADS:], each_tile(hb[:, HEADS:], HEADS), ALU.add))
            start(dve.tensor_scalar(gt[:, 4], gt[:, 1], -1.0, None, ALU.mult))
            start(dve.tensor_tensor(gt[:, 5], gt[:, 4], gt[:, 1], ALU.max))
            dve.wait_ge(act0, 3)
            start(dve.tensor_scalar(gt[:, 3], gt[:, 2], 0.5, 0.5, ALU.mult, ALU.add))
            dve.wait_ge(act0, 6)
            start(dve.scalar_tensor_tensor(gt[:, 8], gt[:, 1], 0.0, gt[:, 7], ALU.max, ALU.add))
            start(dve.scalar_tensor_tensor(th_(9), th_(8), -1.0, each_tile(ast[:, 0:HEADS], HEADS), ALU.mult, ALU.mult))
            assert n0[0] == DVE_G
            dve.wait_ge(cum_ps, 1)
            start(dve.tensor_copy(gt[:, 10], bank[1][:, 0:32]))
            start(dve.tensor_copy(gt[:, 11], bank[1][:, 32:64]))
            start(dve.tensor_tensor(gt[:, 12], gt[:, 11], gt[:, 10], ALU.subtract))
            assert n0[0] == DVE_EXPS
            dve.wait_ge(act0, 9)
            start(dve.tensor_tensor(gt[:, 6], gt[:, 3], gt[:, 13], ALU.mult))
            for kind, i in ((BETA, 3), (GC, 10), (EG, 13), (BEG, 6), (EKD, 14), (DEC, 15), (G_, 9)):
                start(dve.tensor_copy(sel[:, :, 4 * kind:4 * kind + 4].rearrange("p h t -> p t h"), th_(i)))
            dve.tensor_copy(taps[:, :], pcol[:, 0:12]).then_inc(gates_ready, 1)

            def body(h, first, last):
                u0 = h * H_UNITS
                st = stages(h, h - 1, u0, first)
                for c in range(H_UNITS):
                    ahead(lo_part, dve, u0, c, last)
                    run(st, (A_STAGES.get(c, []) if c < A_UNITS else D_STAGES.get(c - A_UNITS, [])), first)

            def stages(h, d, u0, first):
                def d_tokens():
                    step(dve.tensor_copy(hs[:, :].unsqueeze(1), sel[:, bass.ds(d, 1), :]), hs_ready, d + 1)
                    dve.wait_ge(d_in_ps, 4 * d + 2)
                    dve.tensor_tensor(four(vb[:, :]), four(m5[:, :]), per_tile(gate(BETA)), ALU.mult).then_inc(vb_ready, 1)
                    dve.wait_ge(d_in_ps, 4 * d + 3)
                    step(dve.tensor_tensor(four(x0[:, :]), four(m6[:, :]), per_tile(gate(GC)), ALU.subtract),
                         x_ready, 3 * d + 1)
                    dve.tensor_scalar(L[:, :], x0[:, :], 0.0, None, ALU.max).then_inc(x_ready, 1)
                    dve.tensor_scalar(QK[:, :], x0[:, :], 0.0, None, ALU.min).then_inc(x_ready, 1)
                    dve.wait_ge(d_in_ps, 4 * d + 4)
                    dve.tensor_copy(dst[:, 4:8], m7[:, 0:4]).then_inc(qss, 1)

                def d_khat():
                    dve.wait_ge(pool_d, 13 * d + 2)
                    dve.tensor_tensor(four(kh[:, :]), four(m4[:, :]), per_tile(dst[:, 16:20]), ALU.mult).then_inc(kh_ready, 1)

                def d_kk():
                    dve.wait_ge(pool_d, 13 * d + 4)
                    dve.wait_ge(kk_ps, 2 * d + 1)
                    dve.tensor_tensor(L[:, :], m5[:, :], L[:, :], ALU.mult).then_inc(L_ready, 1)
                    dve.wait_ge(pool_d, 13 * d + 5)
                    dve.wait_ge(kk_ps, 2 * d + 2)
                    dve.tensor_tensor(QK[:, :], m6[:, :], QK[:, :], ALU.mult).then_inc(L_ready, 1)

                def level_q(i):
                    dve.wait_ge(q_ps, NL * d + i + 1)
                    dve.tensor_tensor(four(Q[:, :]), four(m5[:, :]), each_tile(const(C_MQ + i * P)),
                                      ALU.mult).then_inc(q_made, 1)

                def level_u(i):
                    dve.wait_ge(u_ps, 11 * d + 2 * i + 1)
                    dve.tensor_tensor(TI[:, :], TI[:, :], m6[:, :], ALU.subtract).then_inc(lvl, 1)
                    if i < NL - 1:
                        dve.wait_ge(u_ps, 11 * d + 2 * i + 2)
                        step(dve.tensor_tensor(T[:, :], T[:, :], m7[:, :], ALU.subtract), lvl, 11 * d + 2 * i + 2)

                def new_values(t):
                    dve.wait_ge(vn_ps, 4 * d + t + 1)
                    dve.tensor_copy(vn[:, :], m6[:, 0:P]).then_inc(vn_ready, 1)

                def outputs(t):
                    if t == TT_N - 1:
                        return
                    dve.wait_ge(S_ps, 3 * d + t + 1)
                    if t == 0:
                        o = dve.tensor_copy(S[:, :], m4[:, 0:P])
                    else:
                        o = dve.scalar_tensor_tensor(S[:, :], S[:, :], hs[:, DEC * 4 + t:DEC * 4 + t + 1], m4[:, 0:P],
                                                     ALU.mult, ALU.add)
                    step(o, S_ready, 3 * d + t + 1)

                def d_norm():
                    dve.wait_ge(o_ps, d + 1)
                    dve.tensor_tensor(four(osb[:, :]), four(m7[:, :]), per_tile(dst[:, 20:24]), ALU.mult).then_inc(o_ready, 1)

                def d_turn():
                    dve.wait_ge(oT_ps, d + 1)
                    step(dve.scalar_tensor_tensor(mixT[:, bass.ds(d, 1), :], m4[:, :].unsqueeze(1), wdo_half[:, :],
                                                  zs[:, :].unsqueeze(1), ALU.mult, ALU.mult), mix_done, d + 1)

                def a_tail():
                    dve.wait_ge(oaT_ps, d + 1)
                    dve.tensor_scalar(mixT[:, bass.ds(d + HEADS, 1), :], m7[:, :].unsqueeze(1),
                                      wao[:, :], None, ALU.mult).then_inc(amix, 1)

                def a_norm():
                    tap_cols = pcol[:, 0:96].rearrange("p (n h) -> p n h", h=HEADS)
                    step(dve.tensor_copy(taps[:, :].unsqueeze(2), tap_cols[:, :, bass.ds(h, 1)]), dproj, 17 * h + 1)

                def a_sum():
                    dve.wait_ge(pool_a, 18 * h + 1)
                    dve.reduce_sum(ast[:, 0:8], aT[:, :].rearrange("p (g n) -> p g n", g=8), AXX).then_inc(a_ss, 1)

                def conv(c):
                    n = 17 * h + 2 + 5 * c
                    if c == 3:
                        dve.wait_ge(tanh_done, 4 * h + 4)
                        step(dve.scalar_tensor_tensor(zs[:, :], th[:, :], 1.0, bank[1][:, :], ALU.add, ALU.mult),
                             dproj, 17 * h + 17)
                        return
                    b = bank[c % 2]
                    dve.wait_ge(unit_used, u0 + A_UNITS + 4 * (c + 1))
                    tap = lambda i: taps[:, i * 3 + c:i * 3 + c + 1]
                    step(dve.tensor_scalar(y[:, :], b[:, :], tap(CONV - 1), None, ALU.mult), dproj, n)
                    for s_ in range(1, CONV):
                        step(dve.scalar_tensor_tensor(y[:, s_:], b[:, 0:SEQ - s_], tap(CONV - 1 - s_), y[:, s_:],
                                                      ALU.mult, ALU.add), dproj, n + s_)
                    dve.wait_ge(tanh_done, 4 * h + c + 1)
                    if c == 0 and not first:
                        dve.wait_ge(pool_d, 13 * d + 8)
                    step(dve.scalar_tensor_tensor((qT, kT, vT)[c][:, :], th[:, :], 1.0, y[:, :], ALU.add, ALU.mult),
                         dproj, n + 4)

                def a_score(t):
                    n = (t + 1) * P
                    o = C_NEG + (TT_N - 1 - t) * P
                    dve.wait_ge(s_ps, 4 * h + t + 1)
                    step(dve.tensor_tensor(sm[:, 0:n], bank[2][:, 0:n], K[:, o:o + n], ALU.add),
                         s_max, 8 * h + 2 * t + 1)
                    step(dve.reduce_max(ast[:, 24 + t:25 + t], sm[:, 0:n], AXX), s_max, 8 * h + 2 * t + 2)
                    dve.tensor_scalar(ast[:, 28 + t:29 + t], ast[:, 24 + t:25 + t], -SCALE, None,
                                      ALU.mult).then_inc(sm_ready, 1)

                def a_prob(t):
                    n = (t + 1) * P
                    o = C_CNT + (TT_N - 1 - t) * P
                    dve.wait_ge(ex_ready, 4 * h + t + 1)
                    dve.tensor_tensor_reduce(ex[:, 0:n], ex[:, 0:n], K[:, o:o + n], 1.0, 0.0, ALU.mult, ALU.add,
                                             ast[:, 32 + t:33 + t]).then_inc(p_ready, 1)

                def a_out():
                    dve.wait_ge(p_ready, 4 * h + 4)
                    step(dve.reciprocal(ast[:, 36:40], ast[:, 32:36]), rden, h + 1)
                    dve.wait_ge(pv_ps, 4 * h + 4)
                    dve.tensor_tensor(four(oa[:, :]), four(bank[3][:, :]), per_tile(ast[:, 36:40]),
                                      ALU.mult).then_inc(oa_ready, 1)

                st = dict(d_tokens=d_tokens, d_khat=d_khat, d_kk=d_kk, d_norm=d_norm, d_turn=d_turn, a_tail=a_tail,
                          a_norm=a_norm, a_sum=a_sum, a_out=a_out)
                for i in range(NL):
                    st[f"q{i}"] = lambda i=i: level_q(i)
                    st[f"u{i}"] = lambda i=i: level_u(i)
                for c in range(4):
                    st[f"v{c}"] = lambda c=c: new_values(c)
                    st[f"r{c}"] = lambda c=c: outputs(c)
                    st[f"conv{c}"] = lambda c=c: conv(c)
                    st[f"a_score{c}"] = lambda c=c: a_score(c)
                    st[f"a_prob{c}"] = lambda c=c: a_prob(c)
                return st

            body(0, True, False)
            with dve.Fori(1, HEADS - 1) as h:
                body(h, False, False)
            body(HEADS - 1, False, True)
            st = stages(HEADS, HEADS - 1, None, False)
            for names in list(A_STAGES.values()) + list(D_STAGES.values()):
                run(st, [n for n in names if n[0] in "dquvr" or n in ("a_sq", "a_tail")], False)

            for k in range(KT):
                dve.wait_ge(mhi, k + 1)
                dve.tensor_tensor(in_lo[:, k], mixT[:, k], in_hi[:, k], ALU.subtract).then_inc(mlo, 1)
            for c in range(4):
                for k in range(KT):
                    lo_part(dve, U_OUT, c * KT + k + AHEAD)
                if c == 0:
                    dve.wait_ge(xr_in, 16 * TT_N)
                for t in range(TT_N):
                    if t < TT_N - 1:
                        dve.wait_ge(out_ps, 3 * c + t + 1)
                    else:
                        dve.wait_ge(unit_used, U_OUT + (c + 1) * KT)
                    o = tok[:, t, c * 512:(c + 1) * 512]
                    dve.tensor_tensor(o, o, bank[4 * (c % 2) + t][:, :], ALU.add).then_inc(res, 1)
            dve.wait_ge(ss2, 16)
            dve.reduce_sum(stat[:, 16:20], stat[:, 0:16].rearrange("p (t c) -> p t c", t=TT_N), AXX).then_inc(rstd2, 1)
            for k in range(KT):
                dve.wait_ge(h2hi, k + 1)
                dve.scalar_tensor_tensor(in_lo[:, k], bank[k % 8][:, :], pcol[:, NROW + k:NROW + k + 1], in_hi[:, k],
                                         ALU.mult, ALU.subtract).then_inc(h2lo, 1)

            def ffn_group(g, last):
                with dve.Fori(0, FPG) as f:
                    u0 = U_FFN + g * F_UNITS + f * GU_UNITS
                    F = g * FPG + f
                    for j in range(GU_UNITS):
                        lo_part(dve, u0, j + AHEAD)
                    dve.wait_ge(silu_done, F + 1)
                    dve.wait_ge(unit_used, u0 + GU_UNITS)
                    dve.tensor_tensor(pr[:, :], gs[:, :], bank[1][:, :], ALU.mult).then_inc(prod, 1)
                    dve.wait_ge(acthi, F + 1)
                    dve.tensor_tensor(act_lo[:, bass.ds(f, 1), :], pr[:, :].unsqueeze(1), act_hi[:, bass.ds(f, 1), :],
                                      ALU.subtract).then_inc(actlo, 1)
                u0 = U_FFN + g * F_UNITS + FPG * GU_UNITS
                for c in range(4):
                    for k in range(FPG):
                        j = c * FPG + k
                        if not (last and j >= DN_UNITS - AHEAD):
                            lo_part(dve, u0, j + AHEAD)
                    for t in range(TT_N):
                        if t < TT_N - 1:
                            dve.wait_ge(dn_ps, 12 * g + 3 * c + t + 1)
                        else:
                            dve.wait_ge(unit_used, u0 + (c + 1) * FPG)
                        o = tok[:, t, c * 512:(c + 1) * 512]
                        dve.tensor_tensor(o, o, bank[4 * ((c + 1) % 2) + t][:, :], ALU.add).then_inc(res, 1)
                dve.wait_ge(res, 16 * (g + 2))

            with dve.Fori(0, FG - 1) as g:
                ffn_group(g, False)
            ffn_group(FG - 1, True)

        @block.gpsimd
        def _(pool):
            def step(ins, done, value):
                ins.then_inc(done, 1)
                pool.wait_ge(done, value)

            step(pool.memset(mhalf[:, :], -0.5), pool_set, 1)
            step(pool.memset(ones[:, :], 1.0), pool_set, 2)
            step(pool.memset(epsr[:, 0:4], EPS), pool_set, 3)
            step(pool.memset(epsr[:, 4:], EPS * P), pool_set, 4)
            step(pool.memset(pcount[:, :], float(P)), pool_set, 5)
            n0 = 5
            for t in range(TT_N):
                pool.wait_ge(sumsq, t + 1)
                step(pool.tensor_scalar(stat[:, 4 + t:5 + t], stat[:, t:t + 1], 1.0 / DM, EPS, ALU.mult, ALU.add),
                     pool_set, n0 + t + 1)
                pool.tensor_tensor(stat[:, 8 + t:9 + t], stat[:, 4 + t:5 + t], mhalf[:, 0:1], ALU.pow).then_inc(rstd, 1)

            def body(h, first, last):
                st = stages(h, h - 1, first)
                for c in range(H_UNITS):
                    run(st, (A_STAGES.get(c, []) if c < A_UNITS else D_STAGES.get(c - A_UNITS, [])), first)

            def stages(h, d, first):
                def dstep(i, ins):
                    step(ins, pool_d, 13 * d + i)

                def astep(head, i, ins):
                    step(ins, pool_a, 18 * head + i)

                def rsqrt(one, i, out_, tmp, in_, first_eps):
                    n = out_.shape[-1]
                    one(i, pool.tensor_tensor(tmp, in_, epsr[:, first_eps:first_eps + n], ALU.add))
                    one(i + 1, pool.tensor_tensor(out_, tmp, mhalf[:, 0:out_.shape[-1]], ALU.pow))

                def d_tokens():
                    pool.wait_ge(kss, 4 * d + 4)
                    pool.wait_ge(qss, d + 1)
                    rsqrt(dstep, 1, dst[:, 16:24], dst[:, 8:16], dst[:, 0:8], 0)
                    pool.wait_ge(decay, 3 * d + 1)
                    dstep(3, pool.tensor_tensor(four(L[:, :]), four(L[:, :]), each_tile(const(C_SL)), ALU.mult))
                    dstep(4, pool.tensor_tensor(four(L[:, :]), four(L[:, :]), per_tile(gate(BETA)), ALU.mult))
                    pool.wait_ge(decay, 3 * d + 2)
                    dstep(5, pool.tensor_tensor(four(QK[:, :]), four(QK[:, :]), each_tile(const(C_U)), ALU.mult))
                    pool.wait_ge(kh_ready, d + 1)
                    dstep(6, pool.tensor_tensor(four(kbg[:, :]), four(kh[:, :]), per_tile(gate(BEG)), ALU.mult))
                    dstep(7, pool.tensor_tensor(four(kdec[:, :]), four(kh[:, :]), per_tile(gate(EKD)), ALU.mult))
                    pool.wait_ge(decay, 3 * d + 3)
                    dstep(8, pool.tensor_tensor(qd[:, :], qT[:, :], EGr[:, :], ALU.mult))

                def d_kk():
                    pool.wait_ge(khT_ps, d + 1)
                    pool.wait_ge(L_ready, 2 * d + 1)
                    dstep(9, pool.tensor_tensor(four(T[:, :]), four(L[:, :]), each_tile(const(C_NM1)), ALU.mult))
                    dstep(10, pool.tensor_tensor(four(T[:, :]), four(T[:, :]), each_tile(ident), ALU.add))

                def d_norm():
                    pool.wait_ge(oss, 4 * d + 4)
                    rsqrt(dstep, 11, dst[:, 32:36], dst[:, 28:32], dst[:, 24:28], 4)
                    dstep(13, pool.tensor_tensor(four(osb[:, :]), four(osb[:, :]), per_tile(dst[:, 32:36]), ALU.mult))

                def a_sq():
                    pool.wait_ge(oass, 4 * d + 4)
                    rsqrt(lambda i, o: astep(d, i, o), 16, ast[:, 8:12], ast[:, 4:8], ast[:, 0:4], 4)
                    astep(d, 18, pool.tensor_tensor(four(oa[:, :]), four(oa[:, :]), per_tile(ast[:, 8:12]), ALU.mult))

                def a_norm():
                    pool.wait_ge(qkv_ready, 4 * h + 4)
                    if not first:
                        pool.wait_ge(pv_ps, 4 * h)
                    astep(h, 1, pool.tensor_tensor(four(aT[:, :]), qkv[:, :, 0:2 * P], qkv[:, :, 0:2 * P], ALU.mult))
                    pool.wait_ge(a_ss, h + 1)
                    rsqrt(lambda i, o: astep(h, i, o), 2, ast[:, 16:24], ast[:, 8:16], ast[:, 0:8], 4)
                    cos = cs[:, 0].unsqueeze(2).broadcast_to([P, TT_N, 2, P // 2])
                    sin = cs[:, 1].unsqueeze(2).broadcast_to([P, TT_N, 2, P // 2])
                    a4 = ra[:, :].rearrange("p (t a n) -> p t a n", t=TT_N, a=2)
                    b4 = rb[:, :].rearrange("p (t a n) -> p t a n", t=TT_N, a=2)
                    rn = ast[:, 16:24].rearrange("p (t c) -> p t c", c=2)
                    for c in range(2):
                        X = qkv[:, :, c * P:(c + 1) * P]
                        X4 = X.rearrange("p t (a n) -> p t a n", a=2)
                        i = 4 + 6 * c
                        astep(h, i, pool.tensor_tensor(X, X, rn[:, :, c:c + 1].broadcast_to([P, TT_N, P]), ALU.mult))
                        astep(h, i + 1, pool.tensor_tensor(X, X, each_tile(wqk[:, c, :]), ALU.mult))
                        astep(h, i + 2, pool.tensor_tensor(a4, X4, cos, ALU.mult))
                        astep(h, i + 3, pool.tensor_tensor(b4, X4, sin, ALU.mult))
                        astep(h, i + 4, pool.tensor_tensor(X4[:, :, 0], a4[:, :, 0], b4[:, :, 1], ALU.subtract))
                        astep(h, i + 5, pool.tensor_tensor(X4[:, :, 1], a4[:, :, 1], b4[:, :, 0], ALU.add))

                return dict(d_tokens=d_tokens, d_kk=d_kk, d_norm=d_norm, a_sq=a_sq, a_norm=a_norm)

            pool.wait_ge(act0, 2)
            pool.wait_ge(gates_ready, 1)
            body(0, True, False)
            with pool.Fori(1, HEADS - 1) as h:
                body(h, False, False)
            body(HEADS - 1, False, True)
            st = stages(HEADS, HEADS - 1, False)
            for names in list(A_STAGES.values()) + list(D_STAGES.values()):
                run(st, [n for n in names if n[0] in "dquvr" or n in ("a_sq", "a_tail")], False)

            pool.wait_ge(rstd2, 1)
            step(pool.tensor_scalar(stat[:, 20:24], stat[:, 16:20], 1.0 / DM, EPS, ALU.mult, ALU.add), rstd2, 2)
            step(pool.tensor_tensor(stat[:, 24:28], stat[:, 20:24], mhalf[:, 0:4], ALU.pow), rstd2, 3)
            for k in range(KT):
                if k >= 4:
                    pool.wait_ge(turned2, k - 3)
                pool.tensor_tensor(four(h2c[:, k % 4, :]), tok[:, :, k * P:(k + 1) * P], per_tile(stat[:, 24:28]),
                                   ALU.mult).then_inc(h2, 1)


_INS = ['x', 'positions', 'attn_norm_w', 'w_in', 'conv_w', 'a_log', 'dt_bias', 'delta_out_norm_w', 'q_norm_w',
        'k_norm_w', 'attn_out_norm_w', 'w_out', 'ffn_norm_w', 'w_gate_up', 'w_down']


def kernel(**inputs):
    import concourse.bacc as bacc
    from concourse.bass_utils import run_bass_kernel_spmd as launch

    nc = bacc.Bacc("TRN2", target_bir_lowering=False, num_devices=1)
    arrays, args = {}, []
    for name in _INS:
        a = np.ascontiguousarray(inputs[name])
        arrays[f"in_{name}"] = a
        args.append(nc.dram_tensor(f"in_{name}", a.shape, mybir.dt.from_np(a.dtype), kind="ExternalInput").ap())
    arrays["in_constants"] = constants()
    args.append(nc.dram_tensor("in_constants", (P, C_END), F32, kind="ExternalInput").ap())
    args.append(nc.dram_tensor("out_0", (1, SEQ, DM), F32, kind="ExternalOutput").ap())
    hybrid_layer(nc, *args)
    return launch(nc, [arrays], core_ids=[0]).results[0]["out_0"]
```

```python
from contextlib import ExitStack

import numpy as np

import concourse.bass as bass
from concourse import mybir

F32 = mybir.dt.float32
F32R = mybir.dt.float32r
I32 = mybir.dt.int32
ACT = mybir.ActivationFunctionType
ALU = mybir.AluOpType
AXX = mybir.AxisListType.X

P = 128
SEQ = 512
TT_N = SEQ // P
DM = 2048
KT = DM // P
HEADS = 8
GW = HEADS * P
CONV = 4
FF = ((8 * DM // 3 + 255) // 256) * 256
FT = FF // P
FG = 4
FPG = FT // FG
EPS = 1e-6
SCALE = float(P) ** -0.5
THETA = 10000.0
LEVELS = [2, 4, 8, 16, 32, 64]
NL = len(LEVELS)
NEG = -1e30
DILATED = ((128, 1), (512, 4), (2048, 16))

C_ID, C_U, C_SL, C_NM1, C_MQ = 0, P, 2 * P, 3 * P, 4 * P
C_CNT = C_MQ + NL * P
C_NEG = C_CNT + SEQ
C_FREQ = C_NEG + SEQ
C_END = C_FREQ + P // 2

RING = 4
UNIT = 512
AHEAD = 3
A_N = 3 * P
D_KT = 4
A_UNITS = KT
D_UNITS = 4 * KT // D_KT
H_UNITS = A_UNITS + D_UNITS
O_UNITS = 4 * KT
GU_UNITS = 2 * KT // D_KT
DN_UNITS = 4 * FPG
F_UNITS = FPG * GU_UNITS + DN_UNITS
U_OUT = HEADS * H_UNITS
U_FFN = U_OUT + O_UNITS

BETA, GC, EG, BEG, EKD, DEC, G_ = range(7)

A_STAGES = {1: ["cum", "d_tokens", "a_sq"], 3: ["d_khat"], 4: ["d_kk"], 5: ["a_tail"], 6: ["d_ti"], 7: ["q0"],
            8: ["u0"], 9: ["q1"], 10: ["u1"], 11: ["q2"], 12: ["u2"], 13: ["q3"], 14: ["u3"], 15: ["q4", "a_evac"]}
D_STAGES = {0: ["u4", "a_norm"], 1: ["q5", "a_sum"], 2: ["u5", "a_krot"], 3: ["d_wt", "conv0"],
            4: ["v0", "a_turn", "tanh0"], 5: ["r0", "a_score0", "fin0"], 6: ["v1", "a_mask0"],
            7: ["r1", "a_prob0", "a_score1", "conv1"], 8: ["v2", "a_pv0", "a_mask1", "tanh1"],
            9: ["r2", "a_prob1", "a_score2", "fin1"], 10: ["v3", "a_pv1", "a_mask2"],
            11: ["r3", "a_prob2", "a_score3", "conv2"], 12: ["d_norm", "a_pv2", "a_mask3", "tanh2"],
            13: ["a_prob3", "fin2"], 14: ["a_pv3", "d_turn"], 15: ["a_out", "conv3"]}


UNIT_STEP = "unit"
EPILOGUE = [UNIT_STEP, "d_tokens", "a_sq", UNIT_STEP, UNIT_STEP, "d_khat", UNIT_STEP, "d_kk", UNIT_STEP, UNIT_STEP,
            "a_tail", "d_ti", UNIT_STEP, "q0", UNIT_STEP, "u0", UNIT_STEP, "q1", UNIT_STEP, "u1", UNIT_STEP,
            "q2", "u2", "q3", "u3", "q4", "u4", "q5", "u5", "d_wt", "v0", "r0", "v1", "r1", "v2", "r2", "v3", "r3",
            "d_norm", UNIT_STEP, UNIT_STEP, "d_turn", UNIT_STEP]
OUT_K = [k for k in range(KT) if k % HEADS != HEADS - 1] + [HEADS - 1, 2 * HEADS - 1]
EARLY = KT - 2
assert EPILOGUE.count(UNIT_STEP) == EARLY


SMALL = 11
DVE_SIN, DVE_DB, DVE_ABS, DVE_G, DVE_EXPS, DVE_BEG = 17, 18, 21, 24, 27, 28


def constants():
    c = np.zeros((P, C_END), np.float32)
    i, j = np.arange(P)[:, None], np.arange(P)[None, :]
    c[:, C_ID:C_ID + P] = i == j
    c[:, C_U:C_U + P] = i <= j
    c[:, C_SL:C_SL + P] = i > j
    c[:, C_NM1:C_NM1 + P] = -1.0 * ((i // 2 == j // 2) & (i > j))
    for n, b in enumerate(LEVELS):
        o = C_MQ + n * P
        c[:, o:o + P] = (i // (2 * b) == j // (2 * b)) & ((i // b) % 2 == 0) & ((j // b) % 2 == 1)
    for block in range(TT_N):
        dist = (TT_N - 1 - block) * P + i - j
        count = np.zeros((P, P), np.float32)
        for window, step in DILATED:
            count += (dist >= 0) & (dist <= window) & (dist % step == 0)
        c[:, C_CNT + block * P:C_CNT + (block + 1) * P] = count
        c[:, C_NEG + block * P:C_NEG + (block + 1) * P] = np.where(count > 0, 0.0, NEG)
    half = P // 2
    c[:, C_FREQ:] = (np.float32(THETA) ** (-np.arange(half, dtype=np.float32) / np.float32(half)))[None, :]
    return c


def hybrid_layer(nc, x, positions, attn_norm_w, w_in, conv_w, a_log, dt_bias, delta_out_norm_w, q_norm_w,
                 k_norm_w, attn_out_norm_w, w_out, ffn_norm_w, w_gate_up, w_down, cst, out):
    ctx = ExitStack()

    def sb(name, shape, dt=F32, stack=ctx):
        return stack.enter_context(nc.sbuf_tensor(name, shape, dt))

    def sem(name):
        return ctx.enter_context(nc.semaphore(name))

    with ctx:
        bank = [ctx.enter_context(nc.psum_tensor(f"bank{i}", [P, 512], F32)) for i in range(8)]
        m4, m5, m6, m7 = bank[4:]
        d_bank = bank[0], bank[1], bank[0], m6

        K = sb("K", [P, C_END])
        in_hi = sb("in_hi", [P, KT, SEQ], F32R)
        in_lo = sb("in_lo", [P, KT, SEQ], F32R)
        big = sb("big", [P, KT * SEQ])
        tok = big[:, :].rearrange("p (t d) -> p t d", t=TT_N)
        mixT = big[:, :].rearrange("p (c s) -> p c s", c=KT)
        raw = [sb(f"raw{i}", [P, UNIT]) for i in range(RING)]
        whi = [sb(f"whi{i}", [P, UNIT], F32R) for i in range(RING)]
        wlo = [sb(f"wlo{i}", [P, UNIT], F32R) for i in range(RING)]
        NROW = CONV * 3 * HEADS + KT
        pcol = sb("pcol", [P, NROW + KT + 2])
        wdo_half = sb("wdo_half", [P, 1])
        wao = sb("wao", [P, 1])
        wqk = sb("wqk", [P, 2, P])
        stat = sb("stat", [P, 32])
        mhalf = sb("mhalf", [P, 32])
        ones = sb("ones", [P, P])
        epsr = sb("epsr", [P, 12])
        pcount = sb("pcount", [P, 1])

        mix = ctx.enter_context(ExitStack())

        def mb(name, shape, dt=F32):
            return sb(name, shape, dt, mix)

        sel = mb("sel", [P, HEADS, 28])
        hs = mb("hs", [P, 28])
        cs = mb("cs", [P, 2, TT_N, P // 2])
        qT = mb("qT", [P, SEQ])
        kT = mb("kT", [P, SEQ])
        vT = mb("vT", [P, SEQ])
        zs = mb("zs", [P, SEQ])
        y = mb("y", [P, SEQ])
        th = mb("th", [P, SEQ])
        kh = mb("kh", [P, SEQ])
        T = kh
        kbg = mb("kbg", [P, SEQ])
        kdec = mb("kdec", [P, SEQ])
        vb = mb("vb", [P, SEQ])
        khT = mb("khT", [P, SEQ])
        nwT = khT
        TI = mb("TI", [P, SEQ])
        qsqr = TI
        EGr = TI
        Q = mb("Q", [P, SEQ])
        x0 = Q
        osb = Q
        L = mb("L", [P, SEQ])
        QK = mb("QK", [P, SEQ])
        qd = mb("qd", [P, SEQ])
        S = mb("S", [P, P])
        vn = mb("vn", [P, P])
        dst = mb("dst", [P, 40])
        taps = mb("taps", [P, CONV * 3])
        qkv = mb("qkv", [P, TT_N, 3 * P])
        ra = mb("ra", [P, SEQ])
        sm = ra
        rb = mb("rb", [P, SEQ])
        ex = rb
        aT = mb("aT", [P, 2 * SEQ])
        pT = mb("pT", [P, SEQ])
        oa = pT
        ast = mb("ast", [P, 40])
        junk = mb("junk", [P, SEQ])
        wba_hi = mb("wba_hi", [P, KT * 16], F32R)
        wba_lo = mb("wba_lo", [P, KT * 16], F32R)
        wba = y[:, 0:KT * 16]
        prow = th[0:CONV * 24 + KT, 0:P]
        prow2 = th[0:KT + 2, P:2 * P]
        posi = mb("posi", [P, TT_N], I32)
        gt = kbg[:, :].rearrange("p (n c) -> p n c", c=32)
        hb = mb("hb", [P, 2 * HEADS])

        def four(t, w=P):
            return t.rearrange("p (t d) -> p t d", t=TT_N)

        def per_tile(ap4, w=P):
            return ap4.unsqueeze(2).broadcast_to([P, TT_N, w])

        def each_tile(ap, w=P):
            return ap.unsqueeze(1).broadcast_to([P, TT_N, w])

        def const(o, n=P):
            return K[:, o:o + n]

        def gate(kind):
            return hs[:, kind * 4:kind * 4 + 4]

        def a_rn():
            return ast[:, 16:24].rearrange("p (t c) -> p t c", c=2)

        def rotate(one, eng, i, X, rn, c, a_, b_):
            cos = cs[:, 0].unsqueeze(2).broadcast_to([P, TT_N, 2, P // 2])
            sin = cs[:, 1].unsqueeze(2).broadcast_to([P, TT_N, 2, P // 2])
            X4 = X.rearrange("p t (a n) -> p t a n", a=2)
            a4 = a_.rearrange("p (t a n) -> p t a n", t=TT_N, a=2)
            b4 = b_.rearrange("p (t a n) -> p t a n", t=TT_N, a=2)
            one(i, eng.tensor_tensor(X, X, rn.broadcast_to([P, TT_N, P]), ALU.mult))
            one(i + 1, eng.tensor_tensor(X, X, each_tile(wqk[:, c, :]), ALU.mult))
            one(i + 2, eng.tensor_tensor(a4, X4, cos, ALU.mult))
            one(i + 3, eng.tensor_tensor(b4, X4, sin, ALU.mult))
            one(i + 4, eng.tensor_tensor(X4[:, :, 0], a4[:, :, 0], b4[:, :, 1], ALU.subtract))
            one(i + 5, eng.tensor_tensor(X4[:, :, 1], a4[:, :, 1], b4[:, :, 0], ALU.add))

        ident = const(C_ID)
        conv_tap = lambda tap, c: pcol[:, tap * 24 + c:tap * 24 + c + 1]

        small_in = sem("small_in")
        x_in = [sem(f"x_in{t}") for t in range(TT_N)]
        raw_in = [sem(f"raw_in{i}") for i in range(RING)]
        hi_made = sem("hi_made")
        lo_made = sem("lo_made")
        unit_used = sem("unit_used")
        consts_in = sem("consts_in")
        pool_set = sem("pool_set")
        rows_ps = sem("rows_ps")
        cols_made = sem("cols_made")
        sumsq = sem("sumsq")
        rstd = sem("rstd")
        scaled = sem("scaled")
        turned = sem("turned")
        in_hi_made = sem("in_hi_made")
        in_lo_made = sem("in_lo_made")
        ba_split = sem("ba_split")
        ba_rows = sem("ba_rows")
        ba_ps = sem("ba_ps")
        act0 = sem("act0")
        dve0 = sem("dve0")
        cum_ps = sem("cum_ps")
        gates_ready = sem("gates_ready")
        tanh_done = sem("tanh_done")
        dproj = sem("dproj")
        hs_ready = sem("hs_ready")
        qsq = sem("qsq")
        d_in_ps = sem("d_in_ps")
        kss = sem("kss")
        qss = sem("qss")
        vb_ready = sem("vb_ready")
        x_ready = sem("x_ready")
        decay = sem("decay")
        kh_ready = sem("kh_ready")
        pool_d = sem("pool_d")
        khT_ps = sem("khT_ps")
        khT_ready = sem("khT_ready")
        kk_ps = sem("kk_ps")
        L_ready = sem("L_ready")
        ti_ps = sem("ti_ps")
        ti_ready = sem("ti_ready")
        q_ps = sem("q_ps")
        q_made = sem("q_made")
        u_ps = sem("u_ps")
        lvl = sem("lvl")
        wT_ps = sem("wT_ps")
        wT_ready = sem("wT_ready")
        vn_ps = sem("vn_ps")
        vn_ready = sem("vn_ready")
        S_ps = sem("S_ps")
        S_ready = sem("S_ready")
        o_ps = sem("o_ps")
        o_ready = sem("o_ready")
        oss = sem("oss")
        oT_ps = sem("oT_ps")
        mix_done = sem("mix_done")
        a_ps = sem("a_ps")
        qkv_ready = sem("qkv_ready")
        a_sq = sem("a_sq")
        a_ss = sem("a_ss")
        pool_a = sem("pool_a")
        krot = sem("krot")
        aT_ps = sem("aT_ps")
        aT_ready = sem("aT_ready")
        s_ps = sem("s_ps")
        s_max = sem("s_max")
        sm_ready = sem("sm_ready")
        ex_ready = sem("ex_ready")
        p_ready = sem("p_ready")
        rden = sem("rden")
        pT_ps = sem("pT_ps")
        pT_ready = sem("pT_ready")
        pv_ps = sem("pv_ps")
        oa_ready = sem("oa_ready")
        oass = sem("oass")
        oaT_ps = sem("oaT_ps")
        amix = sem("amix")
        mhi = sem("mhi")
        mlo = sem("mlo")
        xr_in = sem("xr_in")
        out_ps = sem("out_ps")
        res = sem("res")
        ss2 = sem("ss2")
        rstd2 = sem("rstd2")
        h2 = sem("h2")
        turned2 = sem("turned2")
        h2hi = sem("h2hi")
        h2lo = sem("h2lo")
        silu_done = sem("silu_done")
        prod = sem("prod")
        acthi = sem("acthi")
        actlo = sem("actlo")
        dn_ps = sem("dn_ps")
        stored = sem("stored")

        mix.close()
        act_hi = sb("act_hi", [P, FPG, SEQ], F32R)
        act_lo = sb("act_lo", [P, FPG, SEQ], F32R)
        gs = sb("gs", [P, SEQ])
        pr = sb("pr", [P, SEQ])
        h2c = sb("h2c", [P, 4, SEQ])

        x_t = x[0].rearrange("(t p) d -> p t d", p=P)
        out_t = out[0].rearrange("(t p) d -> p t d", p=P)
        win = w_in[0].rearrange("(k p) n -> p k n", p=P)
        wo = w_out[0].rearrange("(k p) n -> p k n", p=P)
        wgu = w_gate_up[0].rearrange("(k p) n -> p k n", p=P)
        wdn = w_down[0].rearrange("(k p) n -> p k n", p=P)
        A0 = 4 * GW + 2 * HEADS

        def value(e, v):
            return v if isinstance(v, int) else e.snap(v)

        def split_wait(u0, c):
            return 4 * u0 + 16 * (c // RING + 1)

        def hi_part(e, u0, c, n=UNIT):
            e.wait_ge(raw_in[c % RING], split_wait(u0, c))
            if not (isinstance(u0, int) and u0 + c < RING):
                e.wait_ge(unit_used, u0 + c - RING + 1)
            e.activation(whi[c % RING][:, 0:n], raw[c % RING][:, 0:n], ACT.Copy).then_inc(hi_made, 1)

        def lo_part(e, u0, c, n=UNIT):
            e.wait_ge(hi_made, u0 + c + 1)
            e.tensor_tensor(wlo[c % RING][:, 0:n], raw[c % RING][:, 0:n], whi[c % RING][:, 0:n],
                            ALU.subtract).then_inc(lo_made, 1)

        def ahead(part, e, u0, c, last=False):
            c += AHEAD
            part(e, u0, c, A_N if c < A_UNITS or (c >= H_UNITS and not last) else UNIT)

        def run(stages, names, skip):
            for name in names:
                if name in stages and not (skip and name[0] in "dquvr") and not (skip and name in ("a_sq", "a_tail")):
                    stages[name]()

        block = ctx.enter_context(nc.Block())

        @block.sync
        def _(sp):
            for t in range(TT_N):
                sp.dma_start(tok[:, t], x_t[:, t]).then_inc(x_in[t], 16)

            def load(u0, c, dst, src):
                if not (isinstance(u0, int) and u0 + c < RING):
                    split = value(sp, u0 + c - RING + 1 + (c == A_UNITS - 1))
                    sp.wait_ge(raw_in[c % RING], 16)
                    sp.wait_ge(lo_made, split)
                sp.dma_start(dst, src).then_inc(raw_in[c % RING], 16)

            def head(h):
                u0 = h * H_UNITS
                for k in range(A_UNITS):
                    src = win[:, k, A0:A0 + 3 * GW].rearrange("p (c n) -> p c n", c=3)[:, :, bass.ds(h * P, P)]
                    load(u0, k, raw[k % RING][:, 0:A_N].rearrange("p (c n) -> p c n", c=3), src)
                for j in range(D_UNITS):
                    c, q = j // 4, j % 4
                    src = win[:, D_KT * q:D_KT * (q + 1), bass.ds(h * P + c * GW, P)]
                    load(u0, A_UNITS + j, raw[j % RING][:, :].rearrange("p (k n) -> p k n", k=D_KT), src)

            head(0)
            with sp.Fori(1, HEADS) as h:
                head(h)
            for c in range(4):
                for k in range(KT):
                    load(U_OUT, c * KT + k, raw[k % RING][:, :], wo[:, OUT_K[k], c * 512:(c + 1) * 512])
            with sp.Fori(0, FG) as g:
                with sp.Fori(0, FPG) as f:
                    u0 = U_FFN + g * F_UNITS + f * GU_UNITS
                    for j in range(GU_UNITS):
                        c, q = j // 4, j % 4
                        src = wgu[:, D_KT * q:D_KT * (q + 1), bass.ds((g * FPG + f) * P + c * FF, P)]
                        load(u0, j, raw[j % RING][:, :].rearrange("p (k n) -> p k n", k=D_KT), src)
                u0 = U_FFN + g * F_UNITS + FPG * GU_UNITS
                for j in range(DN_UNITS):
                    c, k = j // FPG, j % FPG
                    src = wdn[:, bass.ds(g * FPG + k, 1), c * 512:(c + 1) * 512]
                    load(u0, j, raw[j % RING][:, :].rearrange("p (k n) -> p k n", k=1), src)
            for c in range(4):
                for t in range(TT_N):
                    sp.wait_ge(res, FG * 16 + 4 * c + t + 1)
                    sp.dma_start(out_t[:, t, c * 512:(c + 1) * 512],
                                 tok[:, t, c * 512:(c + 1) * 512]).then_inc(stored, 16)
            sp.wait_ge(stored, 16 * 16)

        @block.tensor
        def _(pe):
            def turn(dst_, src_):
                return pe.transpose(dst_, src_, ident)

            def tiles(dst_, lhs, rhs, done):
                for t in range(TT_N):
                    o = pe.matmul(dst_[:, t * P:(t + 1) * P], lhs[:, t * P:(t + 1) * P], rhs[:, t * P:(t + 1) * P],
                                  start=True, stop=True)
                o.then_inc(done, 1)

            def turns(dst_, src_, done):
                for t in range(TT_N):
                    o = turn(dst_[:, t * P:(t + 1) * P], src_[:, t * P:(t + 1) * P])
                o.then_inc(done, 1)

            pe.wait_ge(consts_in, 16)
            pe.wait_ge(small_in, 16 * SMALL)
            pe.transpose(bank[0][:, 0:NROW], prow, ident[0:NROW, 0:NROW]).then_inc(rows_ps, 1)
            pe.transpose(bank[1][:, 0:KT + 2], prow2, ident[0:KT + 2, 0:KT + 2]).then_inc(rows_ps, 1)
            for k in range(KT):
                if k == 0:
                    pe.wait_ge(cols_made, 3)
                    pe.wait_ge(scaled, TT_N)
                if k >= 8:
                    pe.wait_ge(in_lo_made, k - 7)
                for t in range(TT_N):
                    o = turn(bank[k % 8][:, t * P:(t + 1) * P], tok[:, t, k * P:(k + 1) * P])
                o.then_inc(turned, 1)
            pe.wait_ge(in_lo_made, KT)
            pe.wait_ge(ba_split, 2)
            for k in range(KT):
                for n, (a, b) in enumerate(((in_hi, wba_hi), (in_lo, wba_hi), (in_hi, wba_lo))):
                    o = pe.matmul(m4[0:16, :], b[:, k * 16:(k + 1) * 16], a[:, k, :],
                                  start=(k == 0 and n == 0), stop=(k == KT - 1 and n == 2))
            o.then_inc(ba_ps, 1)
            pe.wait_ge(ba_rows, 1)
            for t in range(TT_N):
                o = pe.transpose(m5[:, t * 16:(t + 1) * 16], ra[0:16, t * P:(t + 1) * P], ident[0:16, 0:16])
            o.then_inc(ba_ps, 1)

            def split3(dst_, pairs, start, stop):
                for n, (a, b) in enumerate(pairs):
                    o = pe.matmul(dst_, a, b, start=(start and n == 0), stop=(stop and n == 2))
                return o

            def body(h, first, last):
                d = h - 1
                st = stages(h, d, first)
                u0 = h * H_UNITS
                for k in range(A_UNITS):
                    pe.wait_ge(lo_made, u0 + k + 1)
                    for t in range(TT_N):
                        if k == 0 and not first and t == 0:
                            pe.wait_ge(dproj, 17 * d + 15)
                        if k == 0 and not first and t == 2:
                            pe.wait_ge(sm_ready, 4 * d + 4)
                        if k == 0 and not first and t == 3:
                            pe.wait_ge(oa_ready, d + 1)
                        c = slice(t * P, (t + 1) * P)
                        hi, lo = whi[k % RING][:, 0:A_N], wlo[k % RING][:, 0:A_N]
                        o = split3(bank[t][:, 0:A_N], ((in_hi[:, k, c], hi), (in_hi[:, k, c], lo), (in_lo[:, k, c], hi)),
                                   k == 0, k == KT - 1)
                        if t == TT_N - 1:
                            o.then_inc(unit_used, 1)
                        elif k == KT - 1:
                            o.then_inc(a_ps, 1)
                    run(st, A_STAGES.get(k, []), first)
                for j in range(D_UNITS):
                    c, q = j // 4, j % 4
                    pe.wait_ge(lo_made, u0 + A_UNITS + j + 1)
                    if q == 0:
                        if c < 2:
                            pe.wait_ge(qkv_ready, 4 * h + c + 1)
                        elif c == 2:
                            pe.wait_ge(dproj, 17 * h + 5)
                        elif not first:
                            pe.wait_ge(vn_ready, 4 * d + 4)
                    for kk in range(D_KT):
                        k, w = D_KT * q + kk, slice(kk * P, (kk + 1) * P)
                        hi, lo = whi[j % RING][:, w], wlo[j % RING][:, w]
                        o = split3(d_bank[c][:, :], ((hi, in_hi[:, k]), (hi, in_lo[:, k]), (lo, in_hi[:, k])),
                                   k == 0, k == KT - 1)
                    o.then_inc(unit_used, 1)
                    run(st, D_STAGES.get(j, []), first)

            def stages(h, d, first):
                def cum():
                    pe.wait_ge(dve0, DVE_G)
                    pe.wait_ge(pool_set, 5)
                    pe.matmul(m6[:, 0:32], const(C_U), gt[:, 9], start=True, stop=True)
                    pe.matmul(m6[:, 32:64], ones[:, :], gt[:, 9], start=True, stop=True).then_inc(cum_ps, 1)

                def d_tokens():
                    pe.wait_ge(dproj, 17 * d + 17)
                    turns(m4, kT, d_in_ps)
                    pe.wait_ge(pT_ready, 4 * d + 4)
                    turns(m5, vT, d_in_ps)
                    pe.wait_ge(hs_ready, d + 1)
                    for t in range(TT_N):
                        g = hs[:, G_ * 4 + t:G_ * 4 + t + 1].broadcast_to([P, P])
                        o = pe.matmul(m6[:, t * P:(t + 1) * P], g, const(C_U), start=True, stop=True)
                    o.then_inc(d_in_ps, 1)
                    pe.wait_ge(qsq, d + 1)
                    for t in range(TT_N):
                        o = pe.matmul(m7[:, t:t + 1], qsqr[:, t * P:(t + 1) * P], pcount[:, :], start=True, stop=True)
                    o.then_inc(d_in_ps, 1)

                def d_khat():
                    pe.wait_ge(kh_ready, d + 1)
                    turns(m4, kh, khT_ps)

                def d_kk():
                    pe.wait_ge(khT_ready, d + 1)
                    pe.wait_ge(vb_ready, d + 1)
                    tiles(m5, khT, khT, kk_ps)
                    pe.wait_ge(decay, 3 * d + 3)
                    tiles(m6, khT, qT, kk_ps)

                def d_ti():
                    pe.wait_ge(pool_d, 13 * d + 10)
                    turns(m4, T, ti_ps)

                def level_q(i):
                    if i == 0:
                        pe.wait_ge(ti_ready, d + 1)
                        pe.wait_ge(L_ready, 2 * d + 2)
                    else:
                        pe.wait_ge(lvl, 11 * d + 2 * i)
                    tiles(m5, L, TI, q_ps)

                def level_u(i):
                    pe.wait_ge(q_made, NL * d + i + 1)
                    tiles(m6, T, Q, u_ps)
                    if i < NL - 1:
                        if i == 0:
                            pe.wait_ge(amix, d + 1)
                        tiles(m7, Q, T, u_ps)

                def d_wt():
                    pe.wait_ge(lvl, 11 * d + 11)
                    pe.wait_ge(pool_d, 13 * d + 8)
                    tiles(m5, kbg, TI, wT_ps)

                def new_values(t):
                    c = slice(t * P, (t + 1) * P)
                    if t:
                        pe.wait_ge(wT_ready, d + 1)
                        pe.wait_ge(S_ready, 3 * d + t)
                    o = pe.matmul(m6[:, 0:P], TI[:, c], vb[:, c], start=True, stop=(t == 0))
                    if t:
                        o = pe.matmul(m6[:, 0:P], nwT[:, c], S[:, :], start=False, stop=True)
                    o.then_inc(vn_ps, 1)

                def outputs(t):
                    c = slice(t * P, (t + 1) * P)
                    pe.wait_ge(vn_ready, 4 * d + t + 1)
                    if t:
                        pe.matmul(m7[:, c], qd[:, c], S[:, :], start=True, stop=False)
                    o = pe.matmul(m7[:, c], QK[:, c], vn[:, :], start=(t == 0), stop=True)
                    if t < TT_N - 1:
                        pe.matmul(m4[:, 0:P], kdec[:, c], vn[:, :], start=True, stop=True).then_inc(S_ps, 1)
                    else:
                        o.then_inc(o_ps, 1)

                def d_turn():
                    pe.wait_ge(pool_d, 13 * d + 13)
                    turns(m4, osb, oT_ps)

                def a_tail():
                    pe.wait_ge(pool_a, 12 * d + 12)
                    pe.wait_ge(qss, d + 1)
                    turns(m7, oa, oaT_ps)

                def a_turn():
                    for c, b in ((0, 2), (1, 3)):
                        pe.wait_ge((pool_a, krot)[c], (12 * h + 9, 6 * h + 6)[c])
                        pe.wait_ge(qkv_ready, 4 * h + 3 + c)
                        for t in range(TT_N):
                            o = turn(bank[b][:, t * P:(t + 1) * P], qkv[:, t, c * P:(c + 1) * P])
                        o.then_inc(aT_ps, 1)

                def a_score(t):
                    pe.wait_ge(aT_ready, 2 * h + 2)
                    if t:
                        pe.wait_ge(sm_ready, 4 * h + t)
                    pe.matmul(bank[2][:, 0:(t + 1) * P], aT[:, t * P:(t + 1) * P], aT[:, SEQ:SEQ + (t + 1) * P],
                              start=True, stop=True).then_inc(s_ps, 1)

                def a_prob(t):
                    pe.wait_ge(p_ready, 4 * h + t + 1)
                    if t:
                        pe.wait_ge(pT_ready, 4 * h + t)
                    elif not first:
                        pe.wait_ge(wT_ready, d + 1)
                    for j in range(t + 1):
                        o = turn(m5[:, j * P:(j + 1) * P], ex[:, j * P:(j + 1) * P])
                    o.then_inc(pT_ps, 1)

                def a_pv(t):
                    pe.wait_ge(pT_ready, 4 * h + t + 1)
                    for j in range(t + 1):
                        o = pe.matmul(bank[3][:, t * P:(t + 1) * P], pT[:, j * P:(j + 1) * P],
                                      qkv[:, j, 2 * P:3 * P], start=(j == 0), stop=(j == t))
                    o.then_inc(pv_ps, 1)

                st = dict(d_tokens=d_tokens, d_khat=d_khat, d_kk=d_kk, d_ti=d_ti, d_wt=d_wt, d_turn=d_turn,
                          a_tail=a_tail, a_turn=a_turn)
                if first:
                    st["cum"] = cum
                for i in range(NL):
                    st[f"q{i}"] = lambda i=i: level_q(i)
                    st[f"u{i}"] = lambda i=i: level_u(i)
                for t in range(TT_N):
                    st[f"v{t}"] = lambda t=t: new_values(t)
                    st[f"r{t}"] = lambda t=t: outputs(t)
                    st[f"a_score{t}"] = lambda t=t: a_score(t)
                    st[f"a_prob{t}"] = lambda t=t: a_prob(t)
                    st[f"a_pv{t}"] = lambda t=t: a_pv(t)
                return st

            body(0, True, False)
            with pe.Fori(1, HEADS - 1) as h:
                body(h, False, False)
            body(HEADS - 1, False, True)
            def out_unit(c, i):
                u, k = c * KT + i, OUT_K[i]
                pe.wait_ge(lo_made, U_OUT + u + 1)
                if c == 0:
                    pe.wait_ge(mlo, i + 1)
                for t in range(TT_N):
                    if i == 0:
                        if c == 0 and t == 0:
                            pe.wait_ge(dproj, 17 * (HEADS - 1) + 15)
                        if c == 0 and t == 2:
                            pe.wait_ge(sm_ready, 4 * HEADS)
                        if c == 0 and t == 3:
                            pe.wait_ge(oa_ready, HEADS)
                        if c == 1 and t == 0:
                            pe.wait_ge(mlo, KT)
                        if c >= 2:
                            pe.wait_ge(res, 4 * (c - 2) + t + 1)
                    s_ = slice(t * P, (t + 1) * P)
                    hi, lo = whi[u % RING][:, :], wlo[u % RING][:, :]
                    o = split3(bank[4 * (c % 2) + t][:, :],
                               ((in_hi[:, k, s_], hi), (in_hi[:, k, s_], lo), (in_lo[:, k, s_], hi)),
                               i == 0, i == KT - 1)
                    if t == TT_N - 1:
                        o.then_inc(unit_used, 1)
                    elif i == KT - 1:
                        o.then_inc(out_ps, 1)

            st = stages(HEADS, HEADS - 1, False)
            early = iter(range(EARLY))
            for name in EPILOGUE:
                if name == UNIT_STEP:
                    out_unit(0, next(early))
                else:
                    run(st, [name], False)
            for c in range(4):
                for i in range(EARLY if c == 0 else 0, KT):
                    out_unit(c, i)
            for k in range(KT):
                pe.wait_ge(h2, k + 1)
                if k >= 8:
                    pe.wait_ge(h2lo, k - 7)
                for t in range(TT_N):
                    o = turn(bank[k % 8][:, t * P:(t + 1) * P], h2c[:, k % 4, t * P:(t + 1) * P])
                o.then_inc(turned2, 1)
            pe.wait_ge(h2lo, KT)

            def ffn_group(g):
                with pe.Fori(0, FPG) as f:
                    u0 = U_FFN + g * F_UNITS + f * GU_UNITS
                    F = g * FPG + f
                    pe.wait_ge(res, 16 + 16 * g)
                    for j in range(GU_UNITS):
                        c, q = j // 4, j % 4
                        pe.wait_ge(lo_made, u0 + j + 1)
                        for kk in range(D_KT):
                            k, w = D_KT * q + kk, slice(kk * P, (kk + 1) * P)
                            hi, lo = whi[j % RING][:, w], wlo[j % RING][:, w]
                            o = split3(bank[c][:, :], ((hi, in_hi[:, k]), (hi, in_lo[:, k]), (lo, in_hi[:, k])),
                                       k == 0, k == KT - 1)
                        o.then_inc(unit_used, 1)
                u0 = U_FFN + g * F_UNITS + FPG * GU_UNITS
                for c in range(4):
                    for k in range(FPG):
                        j = c * FPG + k
                        pe.wait_ge(lo_made, u0 + j + 1)
                        if c == 0:
                            pe.wait_ge(actlo, g * FPG + k + 1)
                        for t in range(TT_N):
                            if k == 0 and c >= 2:
                                pe.wait_ge(res, 16 + 16 * g + 4 * (c - 2) + t + 1)
                            s_ = slice(t * P, (t + 1) * P)
                            hi, lo = whi[j % RING][:, :], wlo[j % RING][:, :]
                            o = split3(bank[4 * ((c + 1) % 2) + t][:, :],
                                       ((act_hi[:, k, s_], hi), (act_hi[:, k, s_], lo), (act_lo[:, k, s_], hi)),
                                       k == 0, k == FPG - 1)
                            if t == TT_N - 1:
                                o.then_inc(unit_used, 1)
                            elif k == FPG - 1:
                                o.then_inc(dn_ps, 1)

            with pe.Fori(0, FG) as g:
                ffn_group(g)

        @block.scalar
        def _(act):
            for dst_, src_ in ((prow[0:CONV * 24], conv_w[0].rearrange("t (c n) -> (t c) n", n=P)),
                               (prow[CONV * 24:NROW], attn_norm_w[0].rearrange("(c n) -> c n", n=P)),
                               (prow2[0:KT], ffn_norm_w[0].rearrange("(c n) -> c n", n=P)),
                               (prow2[KT:KT + 1], delta_out_norm_w), (prow2[KT + 1:KT + 2], attn_out_norm_w)):
                act.dma_start(dst_, src_).then_inc(small_in, 16)
            act.dma_start(K[:, :], cst).then_inc(consts_in, 16)
            act.dma_start(wba.rearrange("p (k n) -> p k n", k=KT), win[:, :, 4 * GW:A0]).then_inc(small_in, 16)
            for dst_, src_ in ((wqk[:, 0, :], q_norm_w), (wqk[:, 1, :], k_norm_w), (hb[:, 0:HEADS], a_log),
                               (hb[:, HEADS:], dt_bias)):
                act.dma_start(dst_, src_.broadcast_to([P, dst_.shape[-1]])).then_inc(small_in, 16)
            act.dma_start(posi[:, :], positions[0].rearrange("(t p) -> p t", p=P),
                          allow_slow_non_contiguous=True).then_inc(small_in, 16)

            for t in range(TT_N):
                act.wait_ge(x_in[t], 16)
                act.activation(in_lo[:, 4 * t:4 * t + 4, :], tok[:, t].rearrange("p (a b) -> p a b", a=4), ACT.Square,
                               accum_out=stat[:, t:t + 1]).then_inc(sumsq, 1)
            act.wait_ge(small_in, 16 * SMALL)
            act.activation(wba_hi[:, :], wba, ACT.Copy).then_inc(ba_split, 1)
            act.wait_ge(dve0, DVE_SIN)
            act.activation(cs[:, 1].rearrange("p t n -> p (t n)"), aT[:, 0:256], ACT.Sin).then_inc(act0, 1)
            act.activation(cs[:, 0].rearrange("p t n -> p (t n)"), aT[:, 256:512], ACT.Sin).then_inc(act0, 1)
            act.wait_ge(cols_made, 3)
            for k in range(KT):
                act.wait_ge(turned, k + 1)
                act.activation(in_hi[:, k], bank[k % 8][:, :], ACT.Copy,
                               scale=pcol[:, CONV * 24 + k:CONV * 24 + k + 1]).then_inc(in_hi_made, 1)
            for u in range(AHEAD):
                hi_part(act, 0, u, A_N)
            act.wait_ge(dve0, DVE_DB)
            act.activation(gt[:, 2], gt[:, 0], ACT.Tanh, scale=0.5).then_inc(act0, 1)
            act.wait_ge(dve0, DVE_ABS)
            act.activation(gt[:, 6], gt[:, 5], ACT.Exp, scale=-1.0).then_inc(act0, 1)
            act.wait_ge(act0, 4)
            act.activation(gt[:, 7], gt[:, 6], ACT.Ln, bias=1.0).then_inc(act0, 1)
            act.activation(ast[:, 0:HEADS], hb[:, 0:HEADS], ACT.Exp).then_inc(act0, 1)
            act.wait_ge(dve0, DVE_EXPS)
            act.activation(gt[:, 13], gt[:, 10], ACT.Exp).then_inc(act0, 1)
            act.activation(gt[:, 14], gt[:, 12], ACT.Exp).then_inc(act0, 1)
            act.activation(gt[:, 15], gt[:, 11], ACT.Exp).then_inc(act0, 1)

            def body(h, first, last):
                u0 = h * H_UNITS
                st = stages(h, h - 1, u0, first)
                for c in range(H_UNITS):
                    ahead(hi_part, act, u0, c, last)
                    run(st, (A_STAGES.get(c, []) if c < A_UNITS else D_STAGES.get(c - A_UNITS, [])), first)

            def stages(h, d, u0, first):
                def d_tokens():
                    act.wait_ge(dproj, 17 * d + 17)
                    act.activation(qsqr[:, :], qT[:, :], ACT.Square).then_inc(qsq, 1)
                    act.wait_ge(d_in_ps, 4 * d + 1)
                    for t in range(TT_N):
                        c = slice(t * P, (t + 1) * P)
                        act.activation(junk[:, c], m4[:, c], ACT.Square, accum_out=dst[:, t:t + 1]).then_inc(kss, 1)
                    act.wait_ge(x_ready, 3 * d + 2)
                    act.activation(L[:, :], L[:, :], ACT.Exp, scale=-1.0).then_inc(decay, 1)
                    act.wait_ge(x_ready, 3 * d + 3)
                    act.activation(QK[:, :], QK[:, :], ACT.Exp).then_inc(decay, 1)
                    act.wait_ge(d_in_ps, 4 * d + 4)
                    act.activation(EGr[:, :], m6[:, :], ACT.Exp).then_inc(decay, 1)

                def a_sq():
                    act.wait_ge(kss, 4 * d + 4)
                    act.wait_ge(oa_ready, d + 1)
                    for t in range(TT_N):
                        c = slice(t * P, (t + 1) * P)
                        act.activation(junk[:, c], oa[:, c], ACT.Square, accum_out=ast[:, t:t + 1]).then_inc(oass, 1)

                def d_khat():
                    act.wait_ge(khT_ps, d + 1)
                    act.activation(khT[:, :], m4[:, :], ACT.Copy).then_inc(khT_ready, 1)

                def d_ti():
                    act.wait_ge(pool_d, 13 * d + 8)
                    act.wait_ge(ti_ps, d + 1)
                    act.activation(TI[:, :], m4[:, :], ACT.Copy).then_inc(ti_ready, 1)

                def d_wt():
                    act.wait_ge(wT_ps, d + 1)
                    act.activation(nwT[:, :], m5[:, :], ACT.Copy, scale=-1.0).then_inc(wT_ready, 1)

                def d_norm():
                    act.wait_ge(oass, 4 * d + 4)
                    act.wait_ge(o_ready, d + 1)
                    for t in range(TT_N):
                        c = slice(t * P, (t + 1) * P)
                        act.activation(junk[:, c], osb[:, c], ACT.Square,
                                       accum_out=dst[:, 24 + t:25 + t]).then_inc(oss, 1)

                def a_evac():
                    if not first:
                        act.wait_ge(pv_ps, 4 * h)
                    for t in range(TT_N):
                        if t < TT_N - 1:
                            act.wait_ge(a_ps, 3 * h + t + 1)
                        else:
                            act.wait_ge(unit_used, u0 + A_UNITS)
                        act.activation(qkv[:, t, :], bank[t][:, 0:A_N], ACT.Copy).then_inc(qkv_ready, 1)

                def conv(c):
                    if c < 3:
                        act.wait_ge(dproj, 17 * h + 5 + 5 * c)
                        act.activation(th[:, :], y[:, :], ACT.Tanh).then_inc(tanh_done, 1)
                    else:
                        act.wait_ge(dproj, 17 * h + 16)
                        act.wait_ge(unit_used, u0 + H_UNITS)
                        act.activation(th[:, :], m6[:, :], ACT.Tanh, scale=0.5).then_inc(tanh_done, 1)

                def a_turn():
                    act.wait_ge(krot, 6 * h + 6)
                    for c in range(2):
                        act.wait_ge(aT_ps, 2 * h + c + 1)
                        act.activation(aT[:, c * SEQ:(c + 1) * SEQ], bank[2 + c][:, :], ACT.Copy).then_inc(aT_ready, 1)

                def a_score(t):
                    n = (t + 1) * P
                    act.wait_ge(sm_ready, 4 * h + t + 1)
                    if t:
                        act.wait_ge(pT_ps, 4 * h + t)
                    act.activation(ex[:, 0:n], sm[:, 0:n], ACT.Exp, scale=SCALE,
                                   bias=ast[:, 28 + t:29 + t]).then_inc(ex_ready, 1)

                def a_prob(t):
                    n = (t + 1) * P
                    act.wait_ge(pT_ps, 4 * h + t + 1)
                    if t:
                        act.wait_ge(pv_ps, 4 * h + t)
                    elif not first:
                        act.wait_ge(oaT_ps, h)
                    act.activation(pT[:, 0:n], m5[:, 0:n], ACT.Copy).then_inc(pT_ready, 1)

                st = dict(d_tokens=d_tokens, a_sq=a_sq, d_khat=d_khat, d_ti=d_ti, d_wt=d_wt, d_norm=d_norm,
                          a_evac=a_evac, a_turn=a_turn)
                for c in range(4):
                    st[f"tanh{c}" if c < 3 else "conv3"] = lambda c=c: conv(c)
                    st[f"a_score{c}"] = lambda c=c: a_score(c)
                    st[f"a_prob{c}"] = lambda c=c: a_prob(c)
                return st

            body(0, True, False)
            with act.Fori(1, HEADS - 1) as h:
                body(h, False, False)
            body(HEADS - 1, False, True)
            def mix_hi(i):
                act.activation(in_hi[:, OUT_K[i]], mixT[:, OUT_K[i]], ACT.Copy).then_inc(mhi, 1)

            act.wait_ge(unit_used, U_OUT)
            act.wait_ge(amix, HEADS - 1)
            act.wait_ge(mix_done, HEADS - 1)
            for i in range(AHEAD):
                mix_hi(i)
            st = stages(HEADS, HEADS - 1, None, False)
            early = iter(range(EARLY))
            for name in EPILOGUE:
                if name == UNIT_STEP:
                    i = next(early)
                    if i + AHEAD < EARLY:
                        mix_hi(i + AHEAD)
                    hi_part(act, U_OUT, i + AHEAD)
                else:
                    run(st, [name], False)
            act.wait_ge(amix, HEADS)
            act.wait_ge(mix_done, HEADS)
            for i in range(EARLY, KT):
                mix_hi(i)
            act.wait_ge(mlo, KT)
            for t in range(TT_N):
                act.dma_start(tok[:, t], x_t[:, t]).then_inc(xr_in, 16)
            for c in range(4):
                for k in range(EARLY if c == 0 else 0, KT):
                    hi_part(act, U_OUT, c * KT + k + AHEAD)
                for t in range(TT_N):
                    act.wait_ge(res, 4 * c + t + 1)
                    act.activation(gs[:, :], tok[:, t, c * 512:(c + 1) * 512], ACT.Square,
                                   accum_out=stat[:, 4 * t + c:4 * t + c + 1]).then_inc(ss2, 1)
                    act.wait_ge(ss2, 4 * c + t + 1)
            for k in range(KT):
                act.wait_ge(turned2, k + 1)
                act.activation(in_hi[:, k], bank[k % 8][:, :], ACT.Copy,
                               scale=pcol[:, NROW + k:NROW + k + 1]).then_inc(h2hi, 1)

            def ffn_group(g, last):
                with act.Fori(0, FPG) as f:
                    u0 = U_FFN + g * F_UNITS + f * GU_UNITS
                    F = g * FPG + f
                    for j in range(GU_UNITS):
                        hi_part(act, u0, j + AHEAD)
                        if j == 3:
                            act.wait_ge(unit_used, u0 + 4)
                            act.activation(gs[:, :], bank[0][:, :], ACT.Silu).then_inc(silu_done, 1)
                    act.wait_ge(prod, F + 1)
                    act.activation(act_hi[:, bass.ds(f, 1), :], pr[:, :].unsqueeze(1), ACT.Copy).then_inc(acthi, 1)
                u0 = U_FFN + g * F_UNITS + FPG * GU_UNITS
                for j in range(DN_UNITS - AHEAD * last):
                    hi_part(act, u0, j + AHEAD)

            with act.Fori(0, FG - 1) as g:
                ffn_group(g, False)
            ffn_group(FG - 1, True)

        @block.vector
        def _(dve):
            def step(ins, done, value):
                ins.then_inc(done, 1)
                dve.wait_ge(done, value)

            n0 = [0]

            def start(ins):
                n0[0] += 1
                step(ins, dve0, n0[0])

            dve.wait_ge(consts_in, 16)
            dve.wait_ge(small_in, 16 * SMALL)
            A, B, C, D = (aT[:, i * 256:(i + 1) * 256] for i in (0, 1, 2, 3))
            a3 = A.rearrange("p (t n) -> p t n", t=TT_N)
            MAGIC = 1.5 * 2.0 ** 23
            two_pi = 2 * np.pi
            c1 = round(two_pi * 2 ** 9) / 2 ** 9
            c2 = round((two_pi - c1) * 2 ** 27) / 2 ** 27
            c3 = two_pi - c1 - c2
            pi_in = 3.1415925
            start(dve.tensor_copy(ast[:, 36:40], posi[:, :]))
            start(dve.tensor_tensor(a3, per_tile(ast[:, 36:40], P // 2), each_tile(K[:, C_FREQ:C_END], P // 2), ALU.mult))
            start(dve.tensor_scalar(B, A, float(1 / two_pi), MAGIC, ALU.mult, ALU.add))
            start(dve.tensor_scalar(B, B, MAGIC, None, ALU.subtract))
            start(dve.tensor_scalar(C, B, 2.0 ** -11, MAGIC, ALU.mult, ALU.add))
            start(dve.tensor_scalar(C, C, MAGIC, 2.0 ** 11, ALU.subtract, ALU.mult))
            start(dve.tensor_tensor(D, B, C, ALU.subtract))
            for turns_, part in ((C, c1), (D, c1), (C, c2), (D, c2), (B, c3)):
                start(dve.scalar_tensor_tensor(A, turns_, -float(part), A, ALU.mult, ALU.add))
            start(dve.tensor_scalar(A, A, -pi_in, pi_in, ALU.max, ALU.min))
            start(dve.tensor_scalar(B, A, float(np.pi / 2), None, ALU.add))
            start(dve.tensor_scalar(C, B, float(np.pi), -float(two_pi), ALU.is_gt, ALU.mult))
            start(dve.tensor_tensor(B, B, C, ALU.add))
            start(dve.tensor_scalar(B, B, -pi_in, pi_in, ALU.max, ALU.min))
            assert n0[0] == DVE_SIN
            dve.wait_ge(rows_ps, 1)
            dve.tensor_scalar(pcol[:, 0:96], bank[0][:, 0:96], 0.5, None, ALU.mult).then_inc(cols_made, 1)
            dve.tensor_copy(pcol[:, 96:NROW], bank[0][:, 96:NROW]).then_inc(cols_made, 1)
            dve.wait_ge(rows_ps, 2)
            step(dve.tensor_copy(pcol[:, NROW:], bank[1][:, 0:KT + 2]), cols_made, 3)
            root = float(P) ** 0.5
            dve.tensor_scalar(wdo_half[:, :], pcol[:, NROW + KT:NROW + KT + 1], 0.5 * root, None,
                              ALU.mult).then_inc(cols_made, 1)
            dve.tensor_scalar(wao[:, :], pcol[:, NROW + KT + 1:NROW + KT + 2], root, None, ALU.mult).then_inc(cols_made, 1)
            dve.tensor_scalar(wqk[:, :, :], wqk[:, :, :], root, None, ALU.mult).then_inc(cols_made, 1)
            dve.wait_ge(ba_split, 1)
            dve.tensor_tensor(wba_lo[:, :], wba, wba_hi[:, :], ALU.subtract).then_inc(ba_split, 1)
            for t in range(TT_N):
                dve.wait_ge(rstd, t + 1)
                dve.tensor_scalar(tok[:, t], tok[:, t], stat[:, 8 + t:9 + t], None, ALU.mult).then_inc(scaled, 1)
            for k in range(KT):
                dve.wait_ge(in_hi_made, k + 1)
                dve.scalar_tensor_tensor(in_lo[:, k], bank[k % 8][:, :], pcol[:, 96 + k:97 + k], in_hi[:, k],
                                         ALU.mult, ALU.subtract).then_inc(in_lo_made, 1)
            for u in range(AHEAD):
                lo_part(dve, 0, u, A_N)
            ba = m5[:, 0:64].rearrange("p (t n) -> p t n", t=TT_N)

            def th_(i):
                return gt[:, i].rearrange("p (t n) -> p t n", t=TT_N)

            dve.wait_ge(ba_ps, 1)
            dve.tensor_copy(ra[0:16, :], m4[0:16, :]).then_inc(ba_rows, 1)
            dve.wait_ge(ba_ps, 2)
            start(dve.tensor_copy(th_(0), ba[:, :, 0:HEADS]))
            start(dve.tensor_tensor(th_(1), ba[:, :, HEADS:], each_tile(hb[:, HEADS:], HEADS), ALU.add))
            start(dve.tensor_scalar(gt[:, 4], gt[:, 1], -1.0, None, ALU.mult))
            start(dve.tensor_tensor(gt[:, 5], gt[:, 4], gt[:, 1], ALU.max))
            dve.wait_ge(act0, 3)
            start(dve.tensor_scalar(gt[:, 3], gt[:, 2], 0.5, 0.5, ALU.mult, ALU.add))
            dve.wait_ge(act0, 6)
            start(dve.scalar_tensor_tensor(gt[:, 8], gt[:, 1], 0.0, gt[:, 7], ALU.max, ALU.add))
            start(dve.scalar_tensor_tensor(th_(9), th_(8), -1.0, each_tile(ast[:, 0:HEADS], HEADS), ALU.mult, ALU.mult))
            assert n0[0] == DVE_G
            dve.wait_ge(cum_ps, 1)
            start(dve.tensor_copy(gt[:, 10], m6[:, 0:32]))
            start(dve.tensor_copy(gt[:, 11], m6[:, 32:64]))
            start(dve.tensor_tensor(gt[:, 12], gt[:, 11], gt[:, 10], ALU.subtract))
            assert n0[0] == DVE_EXPS
            dve.wait_ge(act0, 9)
            start(dve.tensor_tensor(gt[:, 6], gt[:, 3], gt[:, 13], ALU.mult))
            for kind, i in ((BETA, 3), (GC, 10), (EG, 13), (BEG, 6), (EKD, 14), (DEC, 15), (G_, 9)):
                start(dve.tensor_copy(sel[:, :, 4 * kind:4 * kind + 4].rearrange("p h t -> p t h"), th_(i)))
            dve.tensor_copy(taps[:, :], pcol[:, 0:12]).then_inc(gates_ready, 1)

            def body(h, first, last):
                u0 = h * H_UNITS
                st = stages(h, h - 1, u0, first)
                for c in range(H_UNITS):
                    ahead(lo_part, dve, u0, c, last)
                    run(st, (A_STAGES.get(c, []) if c < A_UNITS else D_STAGES.get(c - A_UNITS, [])), first)

            def stages(h, d, u0, first):
                def d_tokens():
                    step(dve.tensor_copy(hs[:, :].unsqueeze(1), sel[:, bass.ds(d, 1), :]), hs_ready, d + 1)
                    dve.wait_ge(d_in_ps, 4 * d + 2)
                    dve.tensor_tensor(four(vb[:, :]), four(m5[:, :]), per_tile(gate(BETA)), ALU.mult).then_inc(vb_ready, 1)
                    dve.wait_ge(d_in_ps, 4 * d + 3)
                    step(dve.tensor_tensor(four(x0[:, :]), four(m6[:, :]), per_tile(gate(GC)), ALU.subtract),
                         x_ready, 3 * d + 1)
                    dve.tensor_scalar(L[:, :], x0[:, :], 0.0, None, ALU.max).then_inc(x_ready, 1)
                    dve.tensor_scalar(QK[:, :], x0[:, :], 0.0, None, ALU.min).then_inc(x_ready, 1)
                    dve.wait_ge(d_in_ps, 4 * d + 4)
                    dve.tensor_copy(dst[:, 4:8], m7[:, 0:4]).then_inc(qss, 1)

                def d_khat():
                    dve.wait_ge(pool_d, 13 * d + 2)
                    dve.tensor_tensor(four(kh[:, :]), four(m4[:, :]), per_tile(dst[:, 16:20]), ALU.mult).then_inc(kh_ready, 1)

                def d_kk():
                    dve.wait_ge(pool_d, 13 * d + 4)
                    dve.wait_ge(kk_ps, 2 * d + 1)
                    dve.tensor_tensor(L[:, :], m5[:, :], L[:, :], ALU.mult).then_inc(L_ready, 1)
                    dve.wait_ge(pool_d, 13 * d + 5)
                    dve.wait_ge(kk_ps, 2 * d + 2)
                    dve.tensor_tensor(QK[:, :], m6[:, :], QK[:, :], ALU.mult).then_inc(L_ready, 1)

                def level_q(i):
                    dve.wait_ge(q_ps, NL * d + i + 1)
                    dve.tensor_tensor(four(Q[:, :]), four(m5[:, :]), each_tile(const(C_MQ + i * P)),
                                      ALU.mult).then_inc(q_made, 1)

                def level_u(i):
                    dve.wait_ge(u_ps, 11 * d + 2 * i + 1)
                    dve.tensor_tensor(TI[:, :], TI[:, :], m6[:, :], ALU.subtract).then_inc(lvl, 1)
                    if i < NL - 1:
                        dve.wait_ge(u_ps, 11 * d + 2 * i + 2)
                        step(dve.tensor_tensor(T[:, :], T[:, :], m7[:, :], ALU.subtract), lvl, 11 * d + 2 * i + 2)

                def new_values(t):
                    dve.wait_ge(vn_ps, 4 * d + t + 1)
                    dve.tensor_copy(vn[:, :], m6[:, 0:P]).then_inc(vn_ready, 1)

                def outputs(t):
                    if t == TT_N - 1:
                        return
                    dve.wait_ge(S_ps, 3 * d + t + 1)
                    if t == 0:
                        o = dve.tensor_copy(S[:, :], m4[:, 0:P])
                    else:
                        o = dve.scalar_tensor_tensor(S[:, :], S[:, :], hs[:, DEC * 4 + t:DEC * 4 + t + 1], m4[:, 0:P],
                                                     ALU.mult, ALU.add)
                    step(o, S_ready, 3 * d + t + 1)

                def d_norm():
                    dve.wait_ge(o_ps, d + 1)
                    dve.tensor_tensor(four(osb[:, :]), four(m7[:, :]), per_tile(dst[:, 20:24]), ALU.mult).then_inc(o_ready, 1)

                def d_turn():
                    dve.wait_ge(oT_ps, d + 1)
                    step(dve.scalar_tensor_tensor(mixT[:, bass.ds(d, 1), :], m4[:, :].unsqueeze(1), wdo_half[:, :],
                                                  zs[:, :].unsqueeze(1), ALU.mult, ALU.mult), mix_done, d + 1)

                def a_tail():
                    dve.wait_ge(oaT_ps, d + 1)
                    dve.tensor_scalar(mixT[:, bass.ds(d + HEADS, 1), :], m7[:, :].unsqueeze(1),
                                      wao[:, :], None, ALU.mult).then_inc(amix, 1)

                def a_norm():
                    tap_cols = pcol[:, 0:96].rearrange("p (n h) -> p n h", h=HEADS)
                    step(dve.tensor_copy(taps[:, :].unsqueeze(2), tap_cols[:, :, bass.ds(h, 1)]), dproj, 17 * h + 1)

                def a_sum():
                    dve.wait_ge(pool_a, 12 * h + 1)
                    dve.reduce_sum(ast[:, 0:8], aT[:, :].rearrange("p (g n) -> p g n", g=8), AXX).then_inc(a_ss, 1)

                def a_krot():
                    dve.wait_ge(pool_a, 12 * h + 3)
                    rotate(lambda i, o: step(o, krot, 6 * h + i), dve, 1, qkv[:, :, P:2 * P], a_rn()[:, :, 1:2], 1,
                           aT[:, 0:SEQ], aT[:, SEQ:])

                def conv(c):
                    n = 17 * h + 2 + 5 * c
                    if c == 3:
                        dve.wait_ge(tanh_done, 4 * h + 4)
                        step(dve.scalar_tensor_tensor(zs[:, :], th[:, :], 1.0, m6[:, :], ALU.add, ALU.mult),
                             dproj, 17 * h + 17)
                        return
                    b = d_bank[c]
                    dve.wait_ge(unit_used, u0 + A_UNITS + 4 * (c + 1))
                    tap = lambda i: taps[:, i * 3 + c:i * 3 + c + 1]
                    step(dve.tensor_scalar(y[:, :], b[:, :], tap(CONV - 1), None, ALU.mult), dproj, n)
                    for s_ in range(1, CONV):
                        step(dve.scalar_tensor_tensor(y[:, s_:], b[:, 0:SEQ - s_], tap(CONV - 1 - s_), y[:, s_:],
                                                      ALU.mult, ALU.add), dproj, n + s_)

                def fin(c):
                    dve.wait_ge(tanh_done, 4 * h + c + 1)
                    if c == 0 and not first:
                        dve.wait_ge(pool_d, 13 * d + 8)
                    step(dve.scalar_tensor_tensor((qT, kT, vT)[c][:, :], th[:, :], 1.0, y[:, :], ALU.add, ALU.mult),
                         dproj, 17 * h + 6 + 5 * c)

                def a_score(t):
                    n = (t + 1) * P
                    o = C_NEG + (TT_N - 1 - t) * P
                    dve.wait_ge(s_ps, 4 * h + t + 1)
                    step(dve.tensor_tensor(sm[:, 0:n], bank[2][:, 0:n], K[:, o:o + n], ALU.add),
                         s_max, 8 * h + 2 * t + 1)
                    step(dve.reduce_max(ast[:, 24 + t:25 + t], sm[:, 0:n], AXX), s_max, 8 * h + 2 * t + 2)
                    dve.tensor_scalar(ast[:, 28 + t:29 + t], ast[:, 24 + t:25 + t], -SCALE, None,
                                      ALU.mult).then_inc(sm_ready, 1)

                def a_mask(t):
                    n = (t + 1) * P
                    o = C_CNT + (TT_N - 1 - t) * P
                    dve.wait_ge(ex_ready, 4 * h + t + 1)
                    dve.tensor_tensor_reduce(ex[:, 0:n], ex[:, 0:n], K[:, o:o + n], 1.0, 0.0, ALU.mult, ALU.add,
                                             ast[:, 32 + t:33 + t]).then_inc(p_ready, 1)

                def a_out():
                    dve.wait_ge(p_ready, 4 * h + 4)
                    step(dve.reciprocal(ast[:, 36:40], ast[:, 32:36]), rden, h + 1)
                    dve.wait_ge(pv_ps, 4 * h + 4)
                    dve.tensor_tensor(four(oa[:, :]), four(bank[3][:, :]), per_tile(ast[:, 36:40]),
                                      ALU.mult).then_inc(oa_ready, 1)

                st = dict(d_tokens=d_tokens, d_khat=d_khat, d_kk=d_kk, d_norm=d_norm, d_turn=d_turn, a_tail=a_tail,
                          a_norm=a_norm, a_sum=a_sum, a_krot=a_krot, a_out=a_out)
                for i in range(NL):
                    st[f"q{i}"] = lambda i=i: level_q(i)
                    st[f"u{i}"] = lambda i=i: level_u(i)
                for c in range(4):
                    st[f"v{c}"] = lambda c=c: new_values(c)
                    st[f"r{c}"] = lambda c=c: outputs(c)
                    st[f"conv{c}"] = lambda c=c: conv(c)
                    st[f"fin{c}"] = lambda c=c: fin(c)
                    st[f"a_score{c}"] = lambda c=c: a_score(c)
                    st[f"a_mask{c}"] = lambda c=c: a_mask(c)
                return st

            body(0, True, False)
            with dve.Fori(1, HEADS - 1) as h:
                body(h, False, False)
            body(HEADS - 1, False, True)
            def mix_lo(i):
                dve.wait_ge(mhi, i + 1)
                dve.tensor_tensor(in_lo[:, OUT_K[i]], mixT[:, OUT_K[i]], in_hi[:, OUT_K[i]],
                                  ALU.subtract).then_inc(mlo, 1)

            for i in range(AHEAD):
                mix_lo(i)
            st = stages(HEADS, HEADS - 1, None, False)
            early = iter(range(EARLY))
            for name in EPILOGUE:
                if name == UNIT_STEP:
                    i = next(early)
                    if i + AHEAD < EARLY:
                        mix_lo(i + AHEAD)
                    lo_part(dve, U_OUT, i + AHEAD)
                else:
                    run(st, [name], False)
            for i in range(EARLY, KT):
                mix_lo(i)
            for c in range(4):
                for k in range(EARLY if c == 0 else 0, KT):
                    lo_part(dve, U_OUT, c * KT + k + AHEAD)
                if c == 0:
                    dve.wait_ge(xr_in, 16 * TT_N)
                for t in range(TT_N):
                    if t < TT_N - 1:
                        dve.wait_ge(out_ps, 3 * c + t + 1)
                    else:
                        dve.wait_ge(unit_used, U_OUT + (c + 1) * KT)
                    o = tok[:, t, c * 512:(c + 1) * 512]
                    dve.tensor_tensor(o, o, bank[4 * (c % 2) + t][:, :], ALU.add).then_inc(res, 1)
            dve.wait_ge(ss2, 16)
            dve.reduce_sum(stat[:, 16:20], stat[:, 0:16].rearrange("p (t c) -> p t c", t=TT_N), AXX).then_inc(rstd2, 1)
            for k in range(KT):
                dve.wait_ge(h2hi, k + 1)
                dve.scalar_tensor_tensor(in_lo[:, k], bank[k % 8][:, :], pcol[:, NROW + k:NROW + k + 1], in_hi[:, k],
                                         ALU.mult, ALU.subtract).then_inc(h2lo, 1)

            def ffn_group(g, last):
                with dve.Fori(0, FPG) as f:
                    u0 = U_FFN + g * F_UNITS + f * GU_UNITS
                    F = g * FPG + f
                    for j in range(GU_UNITS):
                        lo_part(dve, u0, j + AHEAD)
                    dve.wait_ge(silu_done, F + 1)
                    dve.wait_ge(unit_used, u0 + GU_UNITS)
                    dve.tensor_tensor(pr[:, :], gs[:, :], bank[1][:, :], ALU.mult).then_inc(prod, 1)
                    dve.wait_ge(acthi, F + 1)
                    dve.tensor_tensor(act_lo[:, bass.ds(f, 1), :], pr[:, :].unsqueeze(1), act_hi[:, bass.ds(f, 1), :],
                                      ALU.subtract).then_inc(actlo, 1)
                u0 = U_FFN + g * F_UNITS + FPG * GU_UNITS
                for c in range(4):
                    for k in range(FPG):
                        j = c * FPG + k
                        if not (last and j >= DN_UNITS - AHEAD):
                            lo_part(dve, u0, j + AHEAD)
                    for t in range(TT_N):
                        if t < TT_N - 1:
                            dve.wait_ge(dn_ps, 12 * g + 3 * c + t + 1)
                        else:
                            dve.wait_ge(unit_used, u0 + (c + 1) * FPG)
                        o = tok[:, t, c * 512:(c + 1) * 512]
                        dve.tensor_tensor(o, o, bank[4 * ((c + 1) % 2) + t][:, :], ALU.add).then_inc(res, 1)
                dve.wait_ge(res, 16 * (g + 2))

            with dve.Fori(0, FG - 1) as g:
                ffn_group(g, False)
            ffn_group(FG - 1, True)

        @block.gpsimd
        def _(pool):
            def step(ins, done, value):
                ins.then_inc(done, 1)
                pool.wait_ge(done, value)

            step(pool.memset(mhalf[:, :], -0.5), pool_set, 1)
            step(pool.memset(ones[:, :], 1.0), pool_set, 2)
            step(pool.memset(epsr[:, 0:4], EPS), pool_set, 3)
            step(pool.memset(epsr[:, 4:], EPS * P), pool_set, 4)
            step(pool.memset(pcount[:, :], float(P)), pool_set, 5)
            n0 = 5
            for t in range(TT_N):
                pool.wait_ge(sumsq, t + 1)
                step(pool.tensor_scalar(stat[:, 4 + t:5 + t], stat[:, t:t + 1], 1.0 / DM, EPS, ALU.mult, ALU.add),
                     pool_set, n0 + t + 1)
                pool.tensor_tensor(stat[:, 8 + t:9 + t], stat[:, 4 + t:5 + t], mhalf[:, 0:1], ALU.pow).then_inc(rstd, 1)

            def body(h, first, last):
                st = stages(h, h - 1, first)
                for c in range(H_UNITS):
                    run(st, (A_STAGES.get(c, []) if c < A_UNITS else D_STAGES.get(c - A_UNITS, [])), first)

            def stages(h, d, first):
                def dstep(i, ins):
                    step(ins, pool_d, 13 * d + i)

                def astep(head, i, ins):
                    step(ins, pool_a, 12 * head + i)

                def rsqrt(one, i, out_, tmp, in_, first_eps):
                    n = out_.shape[-1]
                    one(i, pool.tensor_tensor(tmp, in_, epsr[:, first_eps:first_eps + n], ALU.add))
                    one(i + 1, pool.tensor_tensor(out_, tmp, mhalf[:, 0:out_.shape[-1]], ALU.pow))

                def d_tokens():
                    pool.wait_ge(kss, 4 * d + 4)
                    pool.wait_ge(qss, d + 1)
                    rsqrt(dstep, 1, dst[:, 16:24], dst[:, 8:16], dst[:, 0:8], 0)
                    pool.wait_ge(decay, 3 * d + 1)
                    dstep(3, pool.tensor_tensor(four(L[:, :]), four(L[:, :]), each_tile(const(C_SL)), ALU.mult))
                    dstep(4, pool.tensor_tensor(four(L[:, :]), four(L[:, :]), per_tile(gate(BETA)), ALU.mult))
                    pool.wait_ge(decay, 3 * d + 2)
                    dstep(5, pool.tensor_tensor(four(QK[:, :]), four(QK[:, :]), each_tile(const(C_U)), ALU.mult))
                    pool.wait_ge(kh_ready, d + 1)
                    dstep(6, pool.tensor_tensor(four(kbg[:, :]), four(kh[:, :]), per_tile(gate(BEG)), ALU.mult))
                    dstep(7, pool.tensor_tensor(four(kdec[:, :]), four(kh[:, :]), per_tile(gate(EKD)), ALU.mult))
                    pool.wait_ge(decay, 3 * d + 3)
                    dstep(8, pool.tensor_tensor(qd[:, :], qT[:, :], EGr[:, :], ALU.mult))

                def d_kk():
                    pool.wait_ge(khT_ps, d + 1)
                    pool.wait_ge(L_ready, 2 * d + 1)
                    dstep(9, pool.tensor_tensor(four(T[:, :]), four(L[:, :]), each_tile(const(C_NM1)), ALU.mult))
                    dstep(10, pool.tensor_tensor(four(T[:, :]), four(T[:, :]), each_tile(ident), ALU.add))

                def d_norm():
                    pool.wait_ge(oss, 4 * d + 4)
                    rsqrt(dstep, 11, dst[:, 32:36], dst[:, 28:32], dst[:, 24:28], 4)
                    dstep(13, pool.tensor_tensor(four(osb[:, :]), four(osb[:, :]), per_tile(dst[:, 32:36]), ALU.mult))

                def a_sq():
                    pool.wait_ge(oass, 4 * d + 4)
                    rsqrt(lambda i, o: astep(d, i, o), 10, ast[:, 8:12], ast[:, 4:8], ast[:, 0:4], 4)
                    astep(d, 12, pool.tensor_tensor(four(oa[:, :]), four(oa[:, :]), per_tile(ast[:, 8:12]), ALU.mult))

                def a_norm():
                    pool.wait_ge(qkv_ready, 4 * h + 4)
                    if not first:
                        pool.wait_ge(pv_ps, 4 * h)
                    astep(h, 1, pool.tensor_tensor(four(aT[:, :]), qkv[:, :, 0:2 * P], qkv[:, :, 0:2 * P], ALU.mult))
                    pool.wait_ge(a_ss, h + 1)
                    rsqrt(lambda i, o: astep(h, i, o), 2, ast[:, 16:24], ast[:, 8:16], ast[:, 0:8], 4)
                    rotate(lambda i, o: astep(h, i, o), pool, 4, qkv[:, :, 0:P], a_rn()[:, :, 0:1], 0, ra[:, :], rb[:, :])

                return dict(d_tokens=d_tokens, d_kk=d_kk, d_norm=d_norm, a_sq=a_sq, a_norm=a_norm)

            pool.wait_ge(act0, 2)
            pool.wait_ge(gates_ready, 1)
            body(0, True, False)
            with pool.Fori(1, HEADS - 1) as h:
                body(h, False, False)
            body(HEADS - 1, False, True)
            st = stages(HEADS, HEADS - 1, False)
            run(st, EPILOGUE, False)

            pool.wait_ge(rstd2, 1)
            step(pool.tensor_scalar(stat[:, 20:24], stat[:, 16:20], 1.0 / DM, EPS, ALU.mult, ALU.add), rstd2, 2)
            step(pool.tensor_tensor(stat[:, 24:28], stat[:, 20:24], mhalf[:, 0:4], ALU.pow), rstd2, 3)
            for k in range(KT):
                if k >= 4:
                    pool.wait_ge(turned2, k - 3)
                pool.tensor_tensor(four(h2c[:, k % 4, :]), tok[:, :, k * P:(k + 1) * P], per_tile(stat[:, 24:28]),
                                   ALU.mult).then_inc(h2, 1)


_INS = ['x', 'positions', 'attn_norm_w', 'w_in', 'conv_w', 'a_log', 'dt_bias', 'delta_out_norm_w', 'q_norm_w',
        'k_norm_w', 'attn_out_norm_w', 'w_out', 'ffn_norm_w', 'w_gate_up', 'w_down']


def kernel(**inputs):
    import concourse.bacc as bacc
    from concourse.bass_utils import run_bass_kernel_spmd as launch

    nc = bacc.Bacc("TRN2", target_bir_lowering=False, num_devices=1)
    arrays, args = {}, []
    for name in _INS:
        a = np.ascontiguousarray(inputs[name])
        arrays[f"in_{name}"] = a
        args.append(nc.dram_tensor(f"in_{name}", a.shape, mybir.dt.from_np(a.dtype), kind="ExternalInput").ap())
    arrays["in_constants"] = constants()
    args.append(nc.dram_tensor("in_constants", (P, C_END), F32, kind="ExternalInput").ap())
    args.append(nc.dram_tensor("out_0", (1, SEQ, DM), F32, kind="ExternalOutput").ap())
    hybrid_layer(nc, *args)
    return launch(nc, [arrays], core_ids=[0]).results[0]["out_0"]
```
